# Optimizing a Trainium2 kernel written in Bass

```python
import jax, jax.numpy as jnp
from jax import lax
import numpy as np

D_MODEL = 1024
BATCH = 1
SEQ = 512
DEPTH = 2

N_MIXERS = 2
N_CONV_LAYERS = (DEPTH + N_MIXERS - 1) // N_MIXERS
N_ATTN_LAYERS = DEPTH // N_MIXERS
NORM_EPS = 1e-6
CONV_WIDTH = 3
HEAD_DIM = 64
HEADS_PER_GROUP = D_MODEL // HEAD_DIM
DILATED_GROUPS = ((128, 1), (512, 4), (2048, 16))
N_ATTN_GROUPS = len(DILATED_GROUPS)
QKV_WIDTH = N_ATTN_GROUPS * 3 * HEADS_PER_GROUP * HEAD_DIM
ROPE_THETA = 10000.0
N_EXPERT_GROUPS = 4
EXPERTS_PER_GROUP = 4
N_EXPERTS = N_EXPERT_GROUPS * EXPERTS_PER_GROUP
FINE_TOP_K = 2
EXPERT_FF = D_MODEL // 2

kernel_name = "hybrid_shortconv_dilated_attn_hmoe"

def rms_norm(x, g):
    xf = x.astype(jnp.float32)
    y = xf * lax.rsqrt(jnp.mean(xf * xf, axis=-1, keepdims=True) + NORM_EPS)
    return (y * g.astype(jnp.float32)).astype(x.dtype)

def rope_tables(positions):
    inv_freq = ROPE_THETA ** (-jnp.arange(0, HEAD_DIM, 2, dtype=jnp.float32) / HEAD_DIM)
    ang = positions.astype(jnp.float32)[..., None] * inv_freq
    return jnp.cos(ang)[:, :, None, :], jnp.sin(ang)[:, :, None, :]

def apply_rope(t, cos, sin):
    tf = t.astype(jnp.float32)
    t1, t2 = jnp.split(tf, 2, axis=-1)
    return jnp.concatenate([t1 * cos - t2 * sin, t2 * cos + t1 * sin], axis=-1).astype(t.dtype)

def short_conv_mixer(x, w_in, conv_w, w_out):
    gate_b, gate_c, h = jnp.split(x @ w_in, 3, axis=-1)
    u = gate_c * h
    conv = lax.conv_general_dilated(
        u, conv_w.reshape(CONV_WIDTH, 1, D_MODEL).astype(u.dtype),
        window_strides=(1,), padding=[(CONV_WIDTH - 1, 0)],
        dimension_numbers=("NWC", "WIO", "NWC"), feature_group_count=D_MODEL)
    return (gate_b * conv) @ w_out

def dilated_window_attention(q, k, v, dilation, n_back):
    B, S, H, Dh = q.shape
    L = S // dilation
    blk = n_back
    nb = -(-L // blk)
    Lp = nb * blk

    def to_strided(t):
        t = t.reshape(B, L, dilation, H, Dh)
        t = jnp.pad(t, ((0, 0), (0, Lp - L), (0, 0), (0, 0), (0, 0)))
        return t.reshape(B, nb, blk, dilation, H, Dh)

    def with_prev(t):
        prev = jnp.pad(t, ((0, 0), (1, 0), (0, 0), (0, 0), (0, 0), (0, 0)))[:, :-1]
        return jnp.concatenate([prev, t], axis=2)

    qs = to_strided(q)
    kb = with_prev(to_strided(k))
    vb = with_prev(to_strided(v))
    scores = jnp.einsum("bnqrhd,bnkrhd->bnrhqk", qs, kb,
                        preferred_element_type=jnp.float32) * (Dh ** -0.5)
    qi = jnp.arange(blk)[:, None]
    ki = jnp.arange(2 * blk)[None, :]
    dist = qi + blk - ki
    band = (dist >= 0) & (dist <= n_back)
    key_valid = (jnp.arange(nb)[:, None] * blk - blk + ki) >= 0
    mask = band[None] & key_valid[:, None, :]
    scores = jnp.where(mask[None, :, None, None], scores, -jnp.inf)
    m = jnp.max(scores, axis=-1, keepdims=True)
    p = jnp.exp(scores - m)
    denom = jnp.sum(p, axis=-1)
    o = jnp.einsum("bnrhqk,bnkrhd->bnqrhd", p, vb.astype(jnp.float32))
    o = o / jnp.transpose(denom, (0, 1, 4, 2, 3))[..., None]
    lse = jnp.transpose(m[..., 0] + jnp.log(denom), (0, 1, 4, 2, 3))
    o = o.reshape(B, Lp, dilation, H, Dh)[:, :L].reshape(B, S, H, Dh)
    lse = lse.reshape(B, Lp, dilation, H)[:, :L].reshape(B, S, H)
    return o, lse

def dilated_attention_mixer(x, w_qkv, w_o, cos, sin):
    B, S, _ = x.shape
    qkv = (x @ w_qkv).reshape(B, S, N_ATTN_GROUPS, 3, HEADS_PER_GROUP, HEAD_DIM)
    outs, lses = [], []
    for g, (window, dilation) in enumerate(DILATED_GROUPS):
        q = apply_rope(qkv[:, :, g, 0], cos, sin)
        k = apply_rope(qkv[:, :, g, 1], cos, sin)
        o, lse = dilated_window_attention(q, k, qkv[:, :, g, 2], dilation, window // dilation)
        outs.append(o)
        lses.append(lse)
    o_all = jnp.stack(outs, axis=3)
    w_grp = jax.nn.softmax(jnp.stack(lses, axis=-1), axis=-1)
    merged = jnp.einsum("bshg,bshgd->bshd", w_grp, o_all).reshape(B, S, D_MODEL)
    return merged.astype(x.dtype) @ w_o

def hierarchical_moe(x, w_coarse, b_coarse, w_fine, b_fine, w_gate, w_up, w_down):
    B, S, D = x.shape
    t = x.reshape(-1, D)
    coarse_logits = (t @ w_coarse).astype(jnp.float32) + b_coarse.astype(jnp.float32)
    coarse_prob = jax.nn.softmax(coarse_logits, axis=-1)
    p_top, g_top = lax.top_k(coarse_prob, 1)
    fine_all = jnp.einsum("nd,gde->nge", t, w_fine).astype(jnp.float32) + b_fine.astype(jnp.float32)
    fine_logits = jnp.take_along_axis(fine_all, g_top[:, :, None], axis=1)[:, 0]
    f_val, f_idx = lax.top_k(fine_logits, FINE_TOP_K)
    gate = p_top * jax.nn.softmax(f_val, axis=-1)
    expert_idx = g_top * EXPERTS_PER_GROUP + f_idx
    combine = jnp.sum(jax.nn.one_hot(expert_idx, N_EXPERTS, dtype=jnp.float32) * gate[..., None], axis=1)
    out = jnp.zeros(t.shape, jnp.float32)
    for e in range(N_EXPERTS):
        h = jax.nn.silu(t @ w_gate[e]) * (t @ w_up[e])
        out = out + combine[:, e:e + 1] * (h @ w_down[e])
    return out.reshape(B, S, D).astype(x.dtype)

def setup_inputs(seed: int = 0) -> dict:
    key = jax.random.key(seed)
    ks = jax.random.split(key, 20)
    f32 = jnp.float32
    nrm = lambda k, shape, s: jax.random.normal(k, shape, f32) * s
    d_s = D_MODEL ** -0.5
    return {
        "x": nrm(ks[0], (BATCH, SEQ, D_MODEL), 1.0),
        "positions": jnp.broadcast_to(jnp.arange(SEQ, dtype=jnp.int32), (BATCH, SEQ)),
        "norm_mix": 1.0 + nrm(ks[1], (DEPTH, D_MODEL), 0.05),
        "norm_ffn": 1.0 + nrm(ks[2], (DEPTH, D_MODEL), 0.05),
        "norm_final": 1.0 + nrm(ks[3], (D_MODEL,), 0.05),
        "conv_w_in": nrm(ks[4], (N_CONV_LAYERS, D_MODEL, 3 * D_MODEL), d_s),
        "conv_w": nrm(ks[5], (N_CONV_LAYERS, CONV_WIDTH, D_MODEL), CONV_WIDTH ** -0.5),
        "conv_w_out": nrm(ks[6], (N_CONV_LAYERS, D_MODEL, D_MODEL), d_s),
        "attn_w_qkv": nrm(ks[7], (N_ATTN_LAYERS, D_MODEL, QKV_WIDTH), d_s),
        "attn_w_o": nrm(ks[8], (N_ATTN_LAYERS, D_MODEL, D_MODEL), d_s),
        "w_coarse": nrm(ks[9], (DEPTH, D_MODEL, N_EXPERT_GROUPS), d_s),
        "b_coarse": nrm(ks[10], (DEPTH, N_EXPERT_GROUPS), 0.01),
        "w_fine": nrm(ks[11], (DEPTH, N_EXPERT_GROUPS, D_MODEL, EXPERTS_PER_GROUP), d_s),
        "b_fine": nrm(ks[12], (DEPTH, N_EXPERT_GROUPS, EXPERTS_PER_GROUP), 0.01),
        "w_gate": nrm(ks[13], (DEPTH, N_EXPERTS, D_MODEL, EXPERT_FF), d_s),
        "w_up": nrm(ks[14], (DEPTH, N_EXPERTS, D_MODEL, EXPERT_FF), d_s),
        "w_down": nrm(ks[15], (DEPTH, N_EXPERTS, EXPERT_FF, D_MODEL), EXPERT_FF ** -0.5),
    }

def reference(x, positions, norm_mix, norm_ffn, norm_final, conv_w_in, conv_w, conv_w_out,
              attn_w_qkv, attn_w_o, w_coarse, b_coarse, w_fine, b_fine, w_gate, w_up, w_down):
    cos, sin = rope_tables(positions)
    h = x
    for i in range(DEPTH):
        hn = rms_norm(h, norm_mix[i])
        j = i // N_MIXERS
        if i % N_MIXERS == 0:
            h = h + short_conv_mixer(hn, conv_w_in[j], conv_w[j], conv_w_out[j])
        else:
            h = h + dilated_attention_mixer(hn, attn_w_qkv[j], attn_w_o[j], cos, sin)
        hn = rms_norm(h, norm_ffn[i])
        h = h + hierarchical_moe(hn, w_coarse[i], b_coarse[i], w_fine[i], b_fine[i],
                                 w_gate[i], w_up[i], w_down[i])
    return rms_norm(h, norm_final)


_drawn_inputs = setup_inputs


def setup_inputs(seed=0):
    import zlib

    import numpy as np

    out = dict(_drawn_inputs(seed))
    spreads = {}
    factors = {'b_coarse': 6.709, 'b_fine': 3.953}
    for name, (base, spread) in spreads.items():
        noise = np.random.default_rng([zlib.crc32(name.encode()), seed]).standard_normal(out[name].shape)
        drawn = base * np.exp(spread * noise) if base else spread * noise
        out[name] = __import__('jax').numpy.asarray(drawn.astype(out[name].dtype))
    for name, factor in factors.items():
        out[name] = (out[name] * factor).astype(out[name].dtype)
    return out
```

```python
from contextlib import ExitStack

import numpy as np

import concourse.bass as bass
from concourse import mybir

ALU = mybir.AluOpType
ACT = mybir.ActivationFunctionType
AX = mybir.AxisListType
F = mybir.dt.float32
FR = mybir.dt.float32r
BF = mybir.dt.bfloat16
I32 = mybir.dt.int32

P = 128
D = 1024
S = 512
NT = S // P
KD = D // P
FF = 512
KF = FF // P
NG, NPG = 4, 4
NE = NG * NPG
HD = 64
NATT = 3
KB = 1024
EPS = 1e-6
NEG = -1e30
CAND = NE * NT
MAX_ITEMS = NE + 2 * S // P
MIN_ITEMS = NE
ITEM_COLS = 32
KEYS = S + 2 * P
SCALE = HD ** -0.5
ROPE_THETA = 10000.0
RAW, SPLIT = 3, 2
MRAW, MSPLIT = 6, 3
U_OUT, U_QKV, U_O, U_END = 12, 16, 52, 56


def build(nc, x, positions, norm_mix, norm_ffn, norm_final, conv_w_in, conv_w, conv_w_out, attn_w_qkv,
          attn_w_o, w_coarse, b_coarse, w_fine, b_fine, w_gate, w_up, w_down, out):
    hn_dram = nc.dram_tensor("hn_rows", (S, D), F, kind="Internal").ap()
    y_dram = nc.dram_tensor("y_rows", (2 * S + 1, D), F, kind="Internal").ap()
    h_dram = nc.dram_tensor("h_rows", (NT, P, D), F, kind="Internal").ap()

    x_v = x.rearrange("b (a r) d -> (b a) (r d)", r=NT)
    out_v = out.rearrange("b (a r) d -> (b a) r d", r=NT)
    pos_v = positions.rearrange("b (a r) -> (b a) r", r=NT)
    gains = [norm_mix[0:1, :], norm_ffn[0:1, :], norm_mix[1:2, :], norm_ffn[1:2, :],
             norm_final.rearrange("(o d) -> o d", o=1)]
    w_in_v = conv_w_in.rearrange("l (p k) n -> (l p) k n", k=KD)
    w_qkv_v = attn_w_qkv.rearrange("l (p k) n -> (l p) k n", k=KD)
    w_out_v = conv_w_out.rearrange("l (k p) n -> (l p) k n", p=P)
    w_o_v = attn_w_o.rearrange("l (k p) n -> (l p) k n", p=P)
    gate_v = w_gate.rearrange("l e (p k) n -> l e p k n", k=KD)
    up_v = w_up.rearrange("l e (p k) n -> l e p k n", k=KD)
    down_v = w_down.rearrange("l e (k p) n -> l e p k n", p=P)

    with ExitStack() as ctx:
        base = -(-nc.sbuf_base // 64) * 64

        def at(name, shape, dt, off):
            return nc.alloc_sbuf_tensor_at(name, shape, dt, offset=base + int(off))

        A, B = 0, 16 * KB
        C = B + 32 * KB
        DR = C + 32 * KB
        E = DR + 24 * KB
        FG = E + int(72.25 * KB)
        G = FG + 16 * KB
        h = at("h", [P, NT, D], F, A)
        oT = at("oT", [P, 12 * D], F, A)
        O_HALF = 10 * D
        xT_hi_all = at("xT_hi_all", [P, KD, S], FR, B)
        xT_lo_all = at("xT_lo_all", [P, KD, S], FR, B + 16 * KB)
        W_hi = [at(f"W_hi{i}", [P, 4, 512], FR, C + 16 * KB * i) for i in range(2)]
        W_lo = [at(f"W_lo{i}", [P, 4, 512], FR, C + 16 * KB * i + 8 * KB) for i in range(2)]
        raw = [at(f"raw{i}", [P, 4, 512], F, DR + 8 * KB * i) for i in range(RAW)]
        c_gate = at("c_gate", [P, 4, 512], F, E)
        conv_o = at("conv_o", [P, 4, 512], F, E + 8 * KB)
        u_pad = at("u_pad", [P, 4, NT, 1 + P], F, E + 16 * KB)
        mixT_hi = at("mixT_hi", [P, KD, S], FR, E + int(24.25 * KB))
        mixT_lo = at("mixT_lo", [P, KD, S], FR, E + int(40.25 * KB))
        m_off = [0, 8, 16, 56.25, 64.25, 24.25]
        m_raw = [at(f"m_raw{i}", [P, 4, 512], F, E + int(o * KB)) for i, o in enumerate(m_off)]
        MW_hi = W_hi + [at("W_hi2", [P, 4, 512], FR, E + int(32.25 * KB))]
        MW_lo = W_lo + [at("W_lo2", [P, 4, 512], FR, E + int(40.25 * KB))]
        x_rows = at("x_rows", [P, D], F, E + int(48.25 * KB))
        y_rows = at("y_rows_sb", [P, D], F, E + int(52.25 * KB))
        y_pick = [at(f"y_pick{i}", [P, D], F, E + int((4 * i if i < 6 else 56.25 + 4 * (i - 6)) * KB))
                  for i in range(2 * NT)]
        qkT = at("qkT", [P, NATT, 2, 4, S], F, E)
        v_all = at("v_all", [P, NATT, NT, 512], F, E + 48 * KB)
        hn = [at(f"hn{i}", [P, D], F, FG + 4 * KB * i) for i in range(2)]
        gain = at("gain", [P, D], F, FG + 8 * KB)
        square_out = at("square_out", [P, D], F, FG + 12 * KB)
        silu_g = at("silu_g", [P, FF], F, FG + 12 * KB)
        act_row = at("act_row", [P, FF], F, FG + 14 * KB)
        qk_rot = at("qk_rot", [P, NT, 512], F, FG)
        rope_a = [at(f"rope_a{i}", [P, 512], F, FG + 8 * KB + 2 * KB * i) for i in range(2)]
        rope_b = [at(f"rope_b{i}", [P, 512], F, FG + 12 * KB + 2 * KB * i) for i in range(2)]
        prob = [at(f"prob{i}", [P, KEYS], F, FG + 3 * KB * i) for i in range(2)]
        probT = at("probT", [P, KEYS], F, FG + 6 * KB)
        q_pad = [at("q_pad0", [P, NATT, S], F, A + 8 * KB), at("q_pad1", [P, NATT, S], F, FG + 9 * KB)]
        rt_off = [E + int(48.25 * KB)]

        def temp(name, shape, dt=F):
            n = 4 * int(np.prod(shape[1:]))
            t = at(name, shape, dt, rt_off[0])
            rt_off[0] += -(-n // 32) * 32
            assert rt_off[0] <= E + int(56.25 * KB)
            return t

        g_off = [G]

        def keep(name, shape, dt=F):
            n = (2 if dt == BF else 4) * int(np.prod(shape[1:]))
            t = at(name, shape, dt, g_off[0])
            g_off[0] += -(-n // 32) * 32
            return t

        ident = keep("ident", [P, P])
        below = keep("below", [P, P])
        ones = keep("ones", [P, P])
        iota_f = keep("iota_f", [P, P])
        mask = keep("mask", [P, NT, KEYS], BF)
        cos_t = keep("cos_t", [P, NT, HD])
        sin_t = keep("sin_t", [P, NT, HD])
        conv_rows = keep("conv_rows", [24, P])
        conv_c = keep("conv_c", [P, 24])
        wc_raw = keep("wc_raw", [P, KD, NG])
        wf_raw = keep("wf_raw", [P, NG, KD, NPG])
        wr_hi = keep("wr_hi", [P, KD, 20], FR)
        wr_lo = keep("wr_lo", [P, KD, 20], FR)
        wr = keep("wr", [P, KD, 20])
        bias_r = keep("bias_r", [P, 20])
        ssq = keep("ssq", [P, NT])
        msq = keep("msq", [P, NT])
        rstd = keep("rstd", [P, NT])
        neghalf = keep("neghalf", [P, 1])
        neg_max = keep("neg_max", [P, 32])
        denom = keep("denom", [P, 32])
        inv_den = keep("inv_den", [P, 32])
        gates = keep("gates", [P, 2, NT])
        dest_list = keep("dest_list", [P, CAND], I32)
        tok_list = keep("tok_list", [P, CAND], I32)
        tok_col = keep("tok_col", [P, 1], I32)
        dest_col = keep("dest_col", [P, 1], I32)
        items = keep("items", [1, ITEM_COLS + 1], I32)
        dest_id = keep("dest_id", [P, 2, NT])
        cand_j = keep("cand_j", [P, 1])
        cand_c = keep("cand_c", [P, 1])
        rank4 = keep("rank4", [P, 4])
        exp512 = keep("exp512", [P, NE])
        assert base + g_off[0] <= nc.sbuf_usable_end, (base + g_off[0], nc.sbuf_usable_end)
        s_off = [E + int(56.25 * KB)]

        def start_temp(name, shape, dt=F):
            t = at(name, shape, dt, s_off[0])
            s_off[0] += -(-4 * int(np.prod(shape[1:])) // 32) * 32
            return t

        pos_i = start_temp("pos_i", [P, NT], I32)
        pos_f = start_temp("pos_f", [P, NT])
        inv_f = start_temp("inv_f", [P, 32])
        ang = start_temp("ang", [P, NT, 32])
        turns = start_temp("turns", [P, 2, NT, 32])
        turns_i = start_temp("turns_i", [P, 2, NT, 32], I32)
        red = start_temp("red", [P, 2, NT, 32])
        trig = start_temp("trig", [P, 2, NT, 32])
        row_i = start_temp("row_i", [P, 1], I32)
        row_m = start_temp("row_m", [P, 1], I32)
        row_mf = start_temp("row_mf", [P, 1])
        dil = start_temp("dil", [P, 32, 4])
        dil0 = start_temp("dil0", [P, 32, 4])
        lg = temp("lg", [P, NT, 20])
        m1 = temp("m1", [P, NT])
        m2 = temp("m2", [P, NT])
        t4 = temp("t4", [P, NT, NG])
        oh_g = temp("oh_g", [P, NT, NG])
        t16 = temp("t16", [P, NT, NG, NPG])
        fsel = temp("fsel", [P, NT, NPG])
        o1 = temp("o1", [P, NT, NPG])
        o2 = temp("o2", [P, NT, NPG])
        e1 = temp("e1", [P, NT, NG, NPG])
        e2 = temp("e2", [P, NT, NG, NPG])
        used = temp("used", [P, NT, NE])
        row_count = temp("row_count", [P, NE])
        row_counts = temp("row_counts", [P, NT, NE])
        ptop = temp("ptop", [P, NT])
        ex = temp("ex", [P, NT])
        rs = temp("rs", [P, NT])
        slot_f = temp("slot_f", [P, 2, NT])
        slot_i = temp("slot_i", [P, 2, NT], I32)
        lane_i = temp("lane_i", [P, 2, NT], I32)
        blk_i = temp("blk_i", [P, 2, NT], I32)
        exp_i = temp("exp_i", [P, 2, NT], I32)
        lane_f = temp("lane_f", [P, 2, NT])
        cand_f = temp("cand_f", [P, 2, NT])
        lane_oh = [temp(f"lane_oh{i}", [P, P]) for i in range(2)]
        blk_oh = [temp(f"blk_oh{i}", [P, CAND]) for i in range(2)]
        valid = temp("valid", [P, 1])
        item_oh = temp("item_oh", [CAND, ITEM_COLS + 1])
        item_v = temp("item_v", [CAND, 1])

        ps = ctx.enter_context(nc.psum_tensor("ps", [P, 8, 512], F))

        def sem(name):
            return ctx.enter_context(nc.semaphore(name))

        x_in, gain_in = sem("x_in"), sem("gain_in")
        sp_passed, pool_passed, dve_passed = sem("sp_passed"), sem("pool_passed"), sem("dve_passed")
        pos_in, conv_in = sem("pos_in"), sem("conv_in")
        router_in = sem("router_in")
        raw_in = [sem(f"raw_in{i}") for i in range(RAW)]
        split_hi, split_lo, unit_done = sem("split_hi"), sem("split_lo"), sem("unit_done")
        pool_step, dve_step, act_step = sem("pool_step"), sem("dve_step"), sem("act_step")
        consts_ready, rows_ready, trig_ready, trig_done = (
            sem("consts_ready"), sem("rows_ready"), sem("trig_ready"), sem("trig_done"))
        conv_t, conv_taps = sem("conv_t"), sem("conv_taps")
        ssq_ready, rstd_ready, hn_ready, h_ready = sem("ssq_ready"), sem("rstd_ready"), sem("hn_ready"), sem("h_ready")
        x_turned, x_hi, x_lo = sem("x_turned"), sem("x_hi"), sem("x_lo")
        block_done, u_ready = sem("block_done"), sem("u_ready")
        gated, mix_hi, mix_lo = sem("gated"), sem("mix_hi"), sem("mix_lo")
        c_ready = sem("c_ready")
        proj_done = sem("proj_done")
        h_saved, h_back, qkv_done = sem("h_saved"), sem("h_back"), sem("qkv_done")
        hn_stored = [sem(f"hn_stored{i}") for i in range(2)]
        out_stored = [sem(f"out_stored{i}") for i in range(2)]
        rope_in, rope_added, qk_turned, qkT_ready, v_ready = (
            sem("rope_in"), sem("rope_added"), sem("qk_turned"), sem("qkT_ready"), sem("v_ready"))
        q_padded, inverted, scaled = sem("q_padded"), sem("inverted"), sem("scaled")
        scored, masked, expd, p_turned, pt_a, pt_b, pv_done, o_stored = (
            sem("scored"), sem("masked"), sem("expd"), sem("p_turned"), sem("pt_a"), sem("pt_b"),
            sem("pv_done"), sem("o_stored"))
        wr_ready, logits_done, ex_in, ex_out, used_ready = (
            sem("wr_ready"), sem("logits_done"), sem("ex_in"), sem("ex_out"), sem("used_ready"))
        pos_done, onehots, list_step, valid_ready, rank_done, item_oh_ready, items_done = (
            sem("pos_done"), sem("onehots"), sem("list_step"), sem("valid_ready"),
            sem("rank_done"), sem("item_oh_ready"), sem("items_done"))
        routed = sem("routed")
        M = []
        for l in range(2):
            M.append({k: sem(f"m{l}_{k}") for k in (
                "hi", "lo", "done", "rows_in", "turned", "xhi", "xlo", "silu", "act", "aturned", "ahi",
                "alo", "y", "ystored", "col", "dest")})
            M[l]["raw_in"] = [sem(f"m{l}_raw_in{i}") for i in range(MRAW)]
            M[l]["pick_in"] = [sem(f"m{l}_pick_in{i}") for i in range(NT)]

        block = ctx.enter_context(nc.Block())

        def product(pe, o, a_hi, a_lo, b_hi, b_lo, first, last):
            pe.matmul(o, a_hi, b_hi, start=first, stop=False)
            pe.matmul(o, a_hi, b_lo, start=False, stop=False)
            return pe.matmul(o, a_lo, b_hi, start=False, stop=last)

        def wait_in_block(eng, c, q, b):
            if b < 3:
                eng.wait_ge(block_done, c * 9 + 3 * q + b + 1)
            else:
                eng.wait_ge(unit_done, c * 6 + SPLIT + 2 * q + 2)

        def wait_qkv(eng, rev, p, r):
            if r < 3:
                eng.wait_ge(qkv_done, rev * 9 + 3 * p + r + 1)
            else:
                eng.wait_ge(unit_done, rev * 6 + SPLIT + U_QKV + 2 * p + 2)

        def out_blocks(j):
            at_ = (j // 2) * O_HALF + (j % 2) * 2 * S
            return oT[:, at_:at_ + 2 * S]

        def later_items(eng):
            return eng.value_load(items[0:1, ITEM_COLS:ITEM_COLS + 1], min_val=MIN_ITEMS - 1, max_val=MAX_ITEMS - 1)

        @block.sync
        def _(sp):
            def dense(uc, rev, src):
                sp.wait_ge(split_lo, rev * 6 + uc + 1)
                sp.sem_inc(sp_passed, 1)
                sp.dma_start(raw[uc % RAW][:, :, :], src).then_inc(raw_in[uc % RAW], 16)

            def unit(l, c, rev, src, view):
                s = M[l]
                sp.wait_ge(s["lo"], rev * 6 + c + 1)
                sp.sem_inc(sp_passed, 1)
                dst = m_raw[c % MRAW][:, :, :]
                if view:
                    dst = dst.rearrange("p a n -> p (a n)").rearrange("p (k n) -> p k n", k=2)
                sp.dma_start(dst, src).then_inc(s["raw_in"][c % MRAW], 16)

            def gate_up(l, e, c, rev):
                for j in range(4):
                    w = (gate_v if j < 2 else up_v)[l, bass.ds(e, 1)].rearrange("e p k n -> (e p) k n")
                    unit(l, c + j, rev, w[:, 4 * (j % 2):4 * (j % 2) + 4, :], False)

            def down(l, e, c, rev):
                for j in range(2):
                    w = down_v[l, bass.ds(e, 1)].rearrange("e p k n -> (e p) k n")
                    unit(l, c + j, rev, w[:, 2 * j:2 * j + 2, :], True)

            def expert(i):
                return sp.value_load(items[0:1, bass.ds(i, 1)], min_val=0, max_val=CAND - 1) % NE

            def moe_weights(l):
                sp.wait_ge(routed, 2 * l + 2)
                later = later_items(sp)
                with sp.Fori(0, later) as i:
                    gate_up(l, expert(i + 1), 4, i)
                    down(l, expert(i), 8, i)
                down(l, expert(later), 4, later)
                sp.wait_ge(M[l]["ystored"], later * 16 + 16)
                sp.sem_inc(sp_passed, 1)
                for r in range(NT):
                    for c in range(2):
                        sp.dma_start(y_pick[2 * r + c][:, :], y_dram[c * S + r * P:c * S + (r + 1) * P, :]
                                     ).then_inc(M[l]["pick_in"][r], 16)

            def norm_gain(k):
                sp.dma_start(gain[:, :], gains[k].to_broadcast([P, D])).then_inc(gain_in, 16)

            def router_weights(l):
                sp.dma_start(wc_raw[:, :, :], w_coarse[l].rearrange("(p k) g -> p k g", k=KD)).then_inc(router_in, 16)
                for g in range(NG):
                    sp.dma_start(wf_raw[:, g, :, :], w_fine[l, g].rearrange("(p k) e -> p k e", k=KD)
                                 ).then_inc(router_in, 16)
                sp.dma_start(bias_r[:, 0:NG], b_coarse[l:l + 1, :].to_broadcast([P, NG])).then_inc(router_in, 16)
                sp.dma_start(bias_r[:, NG:NG + NE], b_fine[l].rearrange("(o g) e -> o (g e)", o=1)
                             .to_broadcast([P, NE])).then_inc(router_in, 16)

            sp.dma_start(h[:, :, :].rearrange("p r d -> p (r d)"), x_v).then_inc(x_in, 16)
            norm_gain(0)
            sp.dma_start(pos_i[:, :], pos_v).then_inc(pos_in, 16)
            sp.dma_start(conv_rows[:, :], conv_w.rearrange("l t (j p) -> (l t j) p", p=P)).then_inc(conv_in, 16)
            router_weights(0)
            with sp.Fori(0, 2) as c:
                for q, col in enumerate((D, 2 * D, 0)):
                    for kh in range(2):
                        dense(2 * q + kh, c, w_in_v[:, 4 * kh:4 * kh + 4, bass.ds(c * 512 + col, 512)])
            sp.wait_ge(hn_ready, 4)
            norm_gain(1)
            for j in range(4):
                dense(U_OUT + j, 0, w_out_v[:, 4 * (j % 2):4 * (j % 2) + 4, 512 * (j // 2):512 * (j // 2) + 512])

            def store_rows(first):
                for r in range(NT):
                    sp.wait_ge(hn_ready, first + r + 1)
                    sp.dma_start(hn_dram[r * P:(r + 1) * P, :], hn[r % 2][:, :]).then_inc(hn_stored[r % 2], 16)

            sp.wait_ge(mix_lo, 8)
            sp.wait_ge(consts_ready, 3)
            gate_up(0, 0, 0, 0)
            store_rows(4)
            norm_gain(2)
            moe_weights(0)
            for r in range(NT):
                sp.wait_ge(h_ready, 4 + r + 1)
                sp.dma_start(h_dram[r], h[:, r, :]).then_inc(h_saved, 16)
            router_weights(1)
            with sp.Fori(0, 2) as s:
                with sp.Fori(0, NATT) as g:
                    for p in range(3):
                        for kh in range(2):
                            dense(U_QKV + 2 * p + kh, s * 3 + g,
                                  w_qkv_v[:, 4 * kh:4 * kh + 4, bass.ds(g * 3 * D + s * 512 + p * D, 512)])
            for j in range(4):
                dense(U_O + j, 0, w_o_v[:, 4 * (j % 2):4 * (j % 2) + 4, 512 * (j // 2):512 * (j // 2) + 512])
            sp.wait_ge(x_lo, 16)
            sp.dma_start(h[:, :, :], h_dram.rearrange("r p d -> p r d")).then_inc(h_back, 16)
            norm_gain(3)
            gate_up(1, 0, 0, 0)
            store_rows(12)
            norm_gain(4)
            moe_weights(1)
            for r in range(NT):
                sp.wait_ge(hn_ready, 16 + r + 1)
                sp.dma_start(out_v[:, r, :], hn[r % 2][:, :]).then_inc(out_stored[r % 2], 16)
            for stored in out_stored:
                sp.wait_ge(stored, 32)

        @block.gpsimd
        def _(pool):
            steps = [0]

            def after(ins):
                steps[0] += 1
                ins.then_inc(pool_step, 1)
                pool.wait_ge(pool_step, steps[0])

            after(pool.memset(ident[:, :], 0.0))
            after(pool.affine_select(out=ident[:, :], in_=ident[:, :], compare_op=ALU.not_equal, fill=1.0, base=0,
                                     pattern=[[-1, P]], channel_multiplier=1))
            pool.memset(ones[:, :], 1.0)
            after(pool.memset(neghalf[:, :], -0.5))
            after(pool.affine_select(out=below[:, :], in_=ones[:, :], compare_op=ALU.is_gt, fill=0.0, base=0,
                                     pattern=[[1, P]], channel_multiplier=-1))
            inv = (np.float32(ROPE_THETA) ** (-np.arange(0, HD, 2, dtype=np.float32) / np.float32(HD))).astype(np.float32)
            for j in range(32):
                last = pool.memset(inv_f[:, j:j + 1], float(inv[j]))
            last.then_inc(consts_ready, 1)
            pool.memset(u_pad[:, :, :, 0:1], 0.0)
            for j in range(4):
                pool.memset(rank4[:, j:j + 1], float(4 - j))
            for e in range(NE):
                pool.memset(exp512[:, e:e + 1], float(S * e))
            pool.iota(iota_f[:, :], pattern=[[1, P]], base=0, channel_multiplier=0, allow_small_or_imprecise_dtypes=True)
            pool.iota(dest_id[:, :, :], pattern=[[S, 2], [P, NT]], base=-2 * S, channel_multiplier=1, allow_small_or_imprecise_dtypes=True)
            pool.iota(cand_c[:, :], pattern=[[0, 1]], base=0, channel_multiplier=1, allow_small_or_imprecise_dtypes=True)
            pool.iota(row_i[:, :], pattern=[[0, 1]], base=0, channel_multiplier=1)
            pool.iota(dil0[:, :, :], pattern=[[0, 32], [1, 4]], base=0, channel_multiplier=0,
                      allow_small_or_imprecise_dtypes=True).then_inc(consts_ready, 1)
            after(pool.memset(mask[:, :, :], 0.0))
            for r in range(NT):
                win = mask[:, r, 0:S].rearrange("p (q b) -> p q b", q=NT)
                after(pool.affine_select(out=win, in_=win, compare_op=ALU.is_ge, fill=NEG, base=r,
                                         pattern=[[-1, NT], [-4, P]], channel_multiplier=4))
                after(pool.affine_select(out=win, in_=win, compare_op=ALU.is_ge, fill=NEG, base=P - r,
                                         pattern=[[1, NT], [4, P]], channel_multiplier=-4))
                last = pool.affine_select(out=mask[:, r, S:S + P], in_=mask[:, r, S:S + P], compare_op=ALU.is_ge,
                                          fill=NEG, base=0, pattern=[[-1, P]], channel_multiplier=1)
            pool.wait_ge(rows_ready, 1)
            for r in range(NT):
                last = pool.affine_select(out=mask[:, r, S + P:KEYS], in_=dil[:, :, :].rearrange("p b q -> p (b q)"),
                                          compare_op=ALU.is_ge, fill=NEG, base=0, pattern=[[-1, P]],
                                          channel_multiplier=1)
            last.then_inc(consts_ready, 1)

            def rstd_tiles(first):
                for r in range(NT):
                    pool.wait_ge(ssq_ready, first + r + 1)
                    after(pool.tensor_scalar(msq[:, r:r + 1], ssq[:, r:r + 1], 1.0 / D, EPS, ALU.mult, ALU.add))
                    pool.tensor_tensor(rstd[:, r:r + 1], msq[:, r:r + 1], neghalf[:, :], ALU.pow).then_inc(rstd_ready, 1)

            def moe_rows(l):
                s = M[l]
                pool.wait_ge(routed, 2 * l + 2)
                for stored in hn_stored:
                    pool.wait_ge(stored, 32 * (l + 1))
                n = later_items(pool) + 1

                def block_of(i):
                    return pool.value_load(items[0:1, bass.ds(i, 1)], min_val=0, max_val=CAND - 1)

                def gather(i):
                    pool.tensor_copy(tok_col[:, :], tok_list[:, bass.ds(block_of(i), 1)]).then_inc(s["col"], 1)
                    pool.wait_ge(s["col"], i + 1)
                    pool.sem_inc(pool_passed, 1)
                    pool.indirect_dma_start(x_rows[:, :], None, hn_dram,
                                            bass.IndirectOffsetOnAxis(ap=tok_col[:, 0:1], axis=0)
                                            ).then_inc(s["rows_in"], 16)

                def store(i):
                    pool.wait_ge(s["y"], i + 2)
                    pool.tensor_copy(dest_col[:, :], dest_list[:, bass.ds(block_of(i), 1)]).then_inc(s["dest"], 1)
                    pool.wait_ge(s["dest"], i + 1)
                    pool.sem_inc(pool_passed, 1)
                    pool.indirect_dma_start(y_dram, bass.IndirectOffsetOnAxis(ap=dest_col[:, 0:1], axis=0),
                                            y_rows[:, :], None).then_inc(s["ystored"], 16)

                gather(0)
                pool.wait_ge(s["turned"], 1)
                gather(1)
                with pool.Fori(1, n) as i:
                    pool.wait_ge(s["turned"], i + 1)
                    gather(i + 1)
                    store(i - 1)
                store(n - 1)

            def rope_sum(g4):
                for r in range(NT):
                    pool.wait_ge(rope_in, g4 + r + 1)
                    pool.wait_ge(qk_turned, g4 + r + 1)
                    pool.tensor_tensor(qk_rot[:, r, :], rope_a[r % 2][:, :], rope_b[r % 2][:, :], ALU.add
                                       ).then_inc(rope_added, 1)

            rstd_tiles(0)
            rstd_tiles(4)
            moe_rows(0)
            rstd_tiles(8)
            with pool.Fori(0, 2) as s:
                with pool.Fori(0, NATT) as g:
                    for p in range(2):
                        rope_sum((s * 6 + g * 2 + p) * 4)
                pool.wait_ge(h_saved, 16 * NT)
                pool.wait_ge(rope_added, s * 24 + 24 + 2)
                pool.wait_ge(qkT_ready, s * 24 + 24 + 2)
                pool.sem_inc(pool_passed, 1)
                pool.memset(q_pad[0][HD:P, :, :], 0.0)
                pool.memset(q_pad[1][0:HD, :, :], 0.0)
                for n in range(8):
                    rows = slice(HD * (n % 2), HD * (n % 2) + HD)
                    if n >= 2:
                        pool.wait_ge(scored, s * 32 + 4 * (n - 1))
                        pool.sem_inc(pool_passed, 1)
                    pool.tensor_copy(q_pad[n % 2][rows, :, :], qkT[rows, :, 0, n // 2, :]).then_inc(q_padded, 1)
            rstd_tiles(12)
            moe_rows(1)
            rstd_tiles(16)

        @block.scalar
        def _(act):
            def hi(uc, rev=0):
                act.wait_ge(raw_in[uc % RAW], rev * 32 + (uc // RAW + 1) * 16)
                act.wait_ge(unit_done, rev * 6 + uc + 1)
                act.activation(W_hi[uc % SPLIT][:, :, :], raw[uc % RAW][:, :, :], ACT.Copy).then_inc(split_hi, 1)

            def square(r, first, ready, count):
                act.wait_ge(ready, count)
                if first + r:
                    act.wait_ge(ssq_ready, first + r)
                act.activation(square_out[:, :], h[:, r, :], ACT.Square,
                               accum_out=ssq[:, r:r + 1]).then_inc(ssq_ready, 1)

            def turn_hi(stage):
                for r in range(NT):
                    b = 2 * (r % 2)
                    act.wait_ge(x_turned, 4 * min(stage, 3) + r + 1)
                    act.activation(xT_hi_all[:, :, r * P:(r + 1) * P],
                                   ps[:, b:b + 2, :].rearrange("p a (k n) -> p (a k) n", n=P), ACT.Copy
                                   ).then_inc(x_hi, 1)

            def m_hi(l, c, rev):
                s = M[l]
                act.wait_ge(s["raw_in"][c % MRAW], rev * 16 + (c // MRAW + 1) * 16)
                act.wait_ge(s["done"], rev * 6 + c + 1)
                act.activation(MW_hi[c % MSPLIT][:, :, :], m_raw[c % MRAW][:, :, :], ACT.Copy).then_inc(s["hi"], 1)

            def experts_begin(l):
                act.wait_ge(unit_done, SPLIT + (U_QKV if l == 0 else U_END))
                for c in range(MSPLIT):
                    m_hi(l, c, 0)
                act.wait_ge(ex_in, 2 * l + 1)
                act.activation(t4[:, :, :], t4[:, :, :], ACT.Exp).then_inc(ex_out, 1)
                act.wait_ge(ex_in, 2 * l + 2)
                act.activation(ex[:, :], ex[:, :], ACT.Exp).then_inc(ex_out, 1)

            def experts(l):
                s = M[l]

                def rows_hi(i):
                    act.wait_ge(s["turned"], i + 1)
                    act.activation(xT_hi_all[:, 0:2, :].rearrange("p a n -> p (a n)"),
                                   ps[:, 2:4, :].rearrange("p a n -> p (a n)"), ACT.Copy).then_inc(s["xhi"], 1)

                def silu(i, unit):
                    act.wait_ge(s["done"], unit + MSPLIT + 1)
                    act.activation(silu_g[:, :], ps[:, 0, :], ACT.Silu).then_inc(s["silu"], 1)

                def act_hi(i):
                    act.wait_ge(s["aturned"], i + 1)
                    act.activation(xT_hi_all[:, 2, :], ps[:, 4, :], ACT.Copy).then_inc(s["ahi"], 1)

                def y_out(i, unit, reused):
                    act.wait_ge(s["done"], unit + MSPLIT + 1)
                    if reused:
                        act.wait_ge(s["ystored"], i * 16)
                    act.activation(y_rows[:, :], ps[:, 5:7, :].rearrange("p a n -> p (a n)"), ACT.Copy
                                   ).then_inc(s["y"], 1)

                rows_hi(0)
                m_hi(l, 3, 0)
                silu(0, 1)
                rows_hi(1)
                m_hi(l, 4, 0)
                m_hi(l, 5, 0)
                act.wait_ge(routed, 2 * l + 2)
                later = later_items(act)

                def step(i, reused):
                    act_hi(i)
                    m_hi(l, 6, i)
                    m_hi(l, 7, i)
                    silu(i + 1, i * 6 + 5)
                    m_hi(l, 8, i)
                    m_hi(l, 9, i)
                    rows_hi(i + 2)
                    m_hi(l, 10, i)
                    m_hi(l, 11, i)
                    y_out(i, i * 6 + 9, reused)

                step(0, False)
                with act.Fori(1, later) as i:
                    step(i, True)
                act_hi(later)
                y_out(later, later * 6 + 5, True)

            act.wait_ge(trig_ready, 1)
            act.activation(trig[:, :, :, :], red[:, :, :, :], ACT.Sin).then_inc(trig_done, 1)
            act.wait_ge(x_in, 16)
            for r in range(NT):
                square(r, 0, x_in, 16)
            turn_hi(0)
            hi(0)
            hi(1)
            with act.Fori(0, 2) as c:
                for q in range(3):
                    hi(2 * q + 2, c)
                    for b in range(4):
                        if q == 0:
                            wait_in_block(act, c, 0, b)
                            act.activation(c_gate[:, b, :], ps[:, b, :], ACT.Copy).then_inc(c_ready, 1)
                        if q == 2:
                            act.wait_ge(gated, c * 4 + b + 1 + 4)
                            act.activation(mixT_hi[:, bass.ds(c * 4 + b, 1), :].rearrange("p a n -> p (a n)"),
                                           conv_o[:, b, :], ACT.Copy).then_inc(mix_hi, 1)
                    hi(2 * q + 3, c)
            hi(14)
            hi(15)
            for r in range(NT):
                square(r, 4, h_ready, r + 1)
            turn_hi(1)
            experts_begin(0)
            experts(0)
            for r in range(NT):
                square(r, 8, h_ready, 4 + r + 1)
            turn_hi(2)
            hi(U_QKV)
            hi(U_QKV + 1)

            def softmax_exp(w, s32):
                act.wait_ge(masked, s32 + w + 1 + 2)
                act.activation(prob[w % 2][:, :], prob[w % 2][:, :], ACT.Exp, bias=neg_max[:, w:w + 1],
                               scale=-1.0, accum_out=denom[:, w:w + 1]).then_inc(expd, 1)

            def store_heads(hb, s):
                act.wait_ge(pv_done, s * 32 + 8 * hb + 8)
                act.activation(oT[:, bass.ds(s * O_HALF + hb * S, S)], ps[:, 6, :], ACT.Copy).then_inc(o_stored, 1)

            with act.Fori(0, 2) as s:
                with act.Fori(0, NATT) as g:
                    for p in range(3):
                        rev = s * 3 + g
                        hi(U_QKV + 2 * p + 2, rev)
                        if p > 0:
                            g4 = (s * 6 + g * 2 + p - 1) * 4
                            for r in range(NT):
                                act.wait_ge(qk_turned, g4 + r + 1 + 4)
                                act.activation(
                                    qkT[:, bass.ds(g, 1), p - 1, :, r * P:(r + 1) * P].rearrange("p a b n -> p (a b) n"),
                                    ps[:, 4 + r % 2, :].rearrange("p (b n) -> p b n", b=4), ACT.Copy
                                ).then_inc(qkT_ready, 1)
                        if p == 2:
                            for r in range(NT):
                                wait_qkv(act, rev, 2, r)
                                act.activation(v_all[:, bass.ds(g, 1), r, :].rearrange("p a n -> p (a n)"),
                                               ps[:, r, :], ACT.Copy).then_inc(v_ready, 1)
                        hi(U_QKV + 2 * p + 3, rev)
                s32 = s * 32
                softmax_exp(0, s32)
                for w in range(32):
                    if w + 1 < 32:
                        softmax_exp(w + 1, s32)
                    if w % 8 == 0 and w:
                        store_heads(w // 8 - 1, s)
                    act.wait_ge(p_turned, s32 + w + 1 + 2)
                    act.activation(probT[:, 0:512], ps[:, 4, :], ACT.Copy).then_inc(pt_a, 1)
                store_heads(3, s)
            act.wait_ge(o_stored, 9)
            for j in range(4):
                act.activation(xT_hi_all[:, 2 * j:2 * j + 2, :].rearrange("p a n -> p (a n)"), out_blocks(j), ACT.Copy
                               ).then_inc(x_hi, 1)
            hi(54)
            hi(55)
            for r in range(NT):
                square(r, 12, h_ready, 8 + r + 1)
            turn_hi(4)
            experts_begin(1)
            experts(1)
            for r in range(NT):
                square(r, 16, h_ready, 12 + r + 1)

        @block.vector
        def _(dve):
            steps = [0]

            def after(ins):
                steps[0] += 1
                ins.then_inc(dve_step, 1)
                dve.wait_ge(dve_step, steps[0])

            def lo(uc, rev=0):
                dve.wait_ge(split_hi, rev * 6 + uc + 1)
                dve.tensor_tensor(W_lo[uc % SPLIT][:, :, :], raw[uc % RAW][:, :, :],
                                  W_hi[uc % SPLIT][:, :, :].bitcast(F), ALU.subtract).then_inc(split_lo, 1)

            def residual_add(which, u0):
                for c in range(2):
                    for r in range(NT):
                        if r < 3:
                            dve.wait_ge(proj_done, 6 * which + 3 * c + r + 1)
                        else:
                            dve.wait_ge(unit_done, SPLIT + u0 + 2 * c + 2)
                        cols = slice(512 * c, 512 * c + 512)
                        ins = dve.tensor_tensor(h[:, r, cols], ps[:, 4 * c + r, :], h[:, r, cols], ALU.add)
                        if c == 1:
                            ins.then_inc(h_ready, 1)

            def norm_rows(k, first, permuted):
                dve.wait_ge(gain_in, 16 * (k + 1))
                for r in range(NT):
                    dve.wait_ge(rstd_ready, first + r + 1)
                    if r >= 2:
                        if first < 16:
                            dve.wait_ge(x_turned, first + r - 1)
                        if first in (4, 12):
                            dve.wait_ge(hn_stored[r % 2], (32 if first == 12 else 0) + 16)
                        if first == 16:
                            dve.wait_ge(out_stored[r % 2], 16)
                    if permuted:
                        o = hn[r % 2][:, :].rearrange("p (k q) -> p k q", k=KD)
                        i0 = h[:, r, :].rearrange("p (q k) -> p k q", k=KD)
                        i1 = gain[:, :].rearrange("p (q k) -> p k q", k=KD)
                    else:
                        o, i0, i1 = hn[r % 2][:, :], h[:, r, :], gain[:, :]
                    dve.scalar_tensor_tensor(out=o, in0=i0, scalar=rstd[:, r:r + 1], in1=i1, op0=ALU.mult,
                                             op1=ALU.mult).then_inc(hn_ready, 1)

            def turn_lo(stage):
                for r in range(NT):
                    b = 2 * (r % 2)
                    dve.wait_ge(x_hi, 4 * stage + r + 1)
                    sl = slice(r * P, (r + 1) * P)
                    dve.tensor_tensor(xT_lo_all[:, :, sl], ps[:, b:b + 2, :].rearrange("p a (k n) -> p (a k) n", n=P),
                                      xT_hi_all[:, :, sl].bitcast(F), ALU.subtract).then_inc(x_lo, 1)

            def router_split(l):
                dve.wait_ge(router_in, 16 * 7 * (l + 1))
                dve.tensor_copy(wr[:, :, 0:NG], wc_raw[:, :, :])
                after(dve.tensor_copy(wr[:, :, NG:20].rearrange("p k (g e) -> p k g e", g=NG),
                                      wf_raw[:, :, :, :].rearrange("p g k e -> p k g e")))
                after(dve.tensor_copy(wr_hi[:, :, :], wr[:, :, :]))
                dve.tensor_tensor(wr_lo[:, :, :], wr[:, :, :], wr_hi[:, :, :].bitcast(F), ALU.subtract
                                  ).then_inc(wr_ready, 1)

            def bc(ap, n):
                return ap.unsqueeze(len(ap.shape)).to_broadcast(list(ap.shape) + [n])

            def first_max(o, vals, mx):
                after(dve.tensor_reduce(mx[:, :], vals, AX.X, ALU.max))
                after(dve.tensor_tensor(o, vals, bc(mx[:, :], 4), ALU.is_equal))
                after(dve.tensor_tensor(o, o, rank4[:, :].unsqueeze(1).to_broadcast([P, NT, 4]), ALU.mult))
                after(dve.tensor_reduce(rs[:, :], o, AX.X, ALU.max))
                after(dve.tensor_tensor(o, o, bc(rs[:, :], 4), ALU.is_equal))

            def route(l):
                dve.wait_ge(logits_done, l + 1)
                after(dve.tensor_tensor(lg[:, :, :], ps[:, 4, 0:80].rearrange("p (r n) -> p r n", r=NT),
                                        bias_r[:, :].unsqueeze(1).to_broadcast([P, NT, 20]), ALU.add))
                coarse = lg[:, :, 0:NG]
                first_max(oh_g[:, :, :], coarse, m1)
                dve.tensor_tensor(t4[:, :, :], coarse, bc(m1[:, :], 4), ALU.subtract).then_inc(ex_in, 1)
                after(dve.tensor_tensor(t16[:, :, :, :], lg[:, :, NG:20].rearrange("p r (g e) -> p r g e", g=NG),
                                        bc(oh_g[:, :, :], NPG), ALU.mult))
                after(dve.tensor_reduce(fsel[:, :, :], t16[:, :, :, :].rearrange("p r g e -> p r e g"), AX.X, ALU.add))
                first_max(o1[:, :, :], fsel[:, :, :], m1)
                after(dve.scalar_tensor_tensor(out=fsel[:, :, :], in0=o1[:, :, :], scalar=NEG, in1=fsel[:, :, :],
                                               op0=ALU.mult, op1=ALU.add))
                first_max(o2[:, :, :], fsel[:, :, :], m2)
                dve.wait_ge(ex_out, 2 * l + 1)
                dve.tensor_tensor(ex[:, :], m2[:, :], m1[:, :], ALU.subtract).then_inc(ex_in, 1)
                after(dve.tensor_reduce(rs[:, :], t4[:, :, :], AX.X, ALU.add))
                after(dve.reciprocal(ptop[:, :], rs[:, :]))
                for o, ee in ((o1, e1), (o2, e2)):
                    last = dve.tensor_tensor(ee[:, :, :, :], bc(oh_g[:, :, :], NPG),
                                             o[:, :, :].unsqueeze(2).to_broadcast([P, NT, NG, NPG]), ALU.mult)
                after(last)
                dve.tensor_tensor(used[:, :, :], e1[:, :, :, :].rearrange("p r g e -> p r (g e)"),
                                  e2[:, :, :, :].rearrange("p r g e -> p r (g e)"), ALU.add).then_inc(used_ready, 1)
                dve.wait_ge(used_ready, 2 * l + 1)
                after(dve.tensor_reduce(row_count[:, :], used[:, :, :].rearrange("p r e -> p e r"), AX.X, ALU.add))
                dve.tensor_copy(row_counts[:, :, :], row_count[:, :].unsqueeze(1).to_broadcast([P, NT, NE])
                                ).then_inc(used_ready, 1)
                dve.wait_ge(ex_out, 2 * l + 2)
                after(dve.tensor_scalar(rs[:, :], ex[:, :], 1.0, None, ALU.add))
                after(dve.reciprocal(rs[:, :], rs[:, :]))
                after(dve.tensor_tensor(gates[:, 0, :], ptop[:, :], rs[:, :], ALU.mult))
                after(dve.tensor_tensor(gates[:, 1, :], gates[:, 0, :], ex[:, :], ALU.mult))
                dve.wait_ge(pos_done, l + 1)
                after(dve.tensor_tensor(used[:, :, :], ps[:, 5, 0:64].rearrange("p (r e) -> p r e", r=NT),
                                        exp512[:, :].unsqueeze(1).to_broadcast([P, NT, NE]), ALU.add))
                for c, ee in enumerate((e1, e2)):
                    ev = ee[:, :, :, :].rearrange("p r g e -> p r (g e)")
                    after(dve.tensor_tensor(ev, ev, used[:, :, :], ALU.mult))
                    last = dve.tensor_reduce(slot_f[:, c, :], ev, AX.X, ALU.add)
                after(last)
                after(dve.tensor_copy(slot_i[:, :, :], slot_f[:, :, :]))
                dve.tensor_scalar(lane_i[:, :, :], slot_i[:, :, :], P - 1, None, ALU.bitwise_and)
                dve.tensor_scalar(exp_i[:, :, :], slot_i[:, :, :], 9, None, ALU.arith_shift_right)
                after(dve.tensor_scalar(blk_i[:, :, :], slot_i[:, :, :], 7, NT - 1, ALU.arith_shift_right,
                                        ALU.bitwise_and))
                dve.tensor_copy(lane_f[:, :, :], lane_i[:, :, :])
                dve.tensor_copy(slot_f[:, :, :], exp_i[:, :, :])
                after(dve.tensor_copy(cand_f[:, :, :], blk_i[:, :, :]))
                after(dve.scalar_tensor_tensor(out=cand_f[:, :, :], in0=cand_f[:, :, :], scalar=float(NE),
                                               in1=slot_f[:, :, :], op0=ALU.mult, op1=ALU.add))
                for n in range(8):
                    r, c = n // 2, n % 2
                    if n >= 2:
                        dve.wait_ge(list_step, 8 * l + n - 1)
                    dve.tensor_scalar(lane_oh[n % 2][:, :], iota_f[:, :], lane_f[:, c, r:r + 1], None, ALU.is_equal)
                    dve.tensor_scalar(blk_oh[n % 2][:, :], iota_f[:, 0:CAND], cand_f[:, c, r:r + 1],
                                      dest_id[:, c, r:r + 1], ALU.is_equal, ALU.mult).then_inc(onehots, 1)
                dve.tensor_scalar(valid[0:CAND, :], ps[0:CAND, 6, 0:1], cand_j[0:CAND, :], None, ALU.is_gt
                                  ).then_inc(valid_ready, 1)
                dve.wait_ge(rank_done, l + 1)
                dve.wait_ge(valid_ready, l + 1)
                after(dve.tensor_copy(item_v[:, :], ps[0:CAND, 7, 0:1]))
                dve.tensor_scalar(item_oh[:, 0:ITEM_COLS], iota_f[0:CAND, 0:ITEM_COLS], item_v[:, :],
                                  valid[0:CAND, :], ALU.is_equal, ALU.mult).then_inc(item_oh_ready, 1)
                dve.wait_ge(list_step, 8 * l + 8)
                after(dve.tensor_scalar(dest_list[:, :], ps[:, 5, 128:128 + CAND], float(2 * S), None, ALU.add))
                dve.tensor_scalar(tok_list[:, :], dest_list[:, :], S - 1, None, ALU.bitwise_and).then_inc(routed, 1)
                dve.wait_ge(items_done, l + 1)
                dve.tensor_scalar(items[:, ITEM_COLS:], ps[0:1, 6, 64 + ITEM_COLS:65 + ITEM_COLS], -1.0, None, ALU.add)
                dve.tensor_copy(items[:, 0:ITEM_COLS], ps[0:1, 6, 64:64 + ITEM_COLS]).then_inc(routed, 1)

            def m_lo(l, c, rev):
                s = M[l]
                dve.wait_ge(s["hi"], rev * 6 + c + 1)
                dve.tensor_tensor(MW_lo[c % MSPLIT][:, :, :], m_raw[c % MRAW][:, :, :],
                                  MW_hi[c % MSPLIT][:, :, :].bitcast(F), ALU.subtract).then_inc(s["lo"], 1)

            def experts(l):
                s = M[l]

                def rows_lo(i):
                    dve.wait_ge(s["xhi"], i + 1)
                    dve.tensor_tensor(xT_lo_all[:, 0:2, :].rearrange("p a n -> p (a n)"),
                                      ps[:, 2:4, :].rearrange("p a n -> p (a n)"),
                                      xT_hi_all[:, 0:2, :].rearrange("p a n -> p (a n)").bitcast(F),
                                      ALU.subtract).then_inc(s["xlo"], 1)

                def act_mul(i, unit):
                    dve.wait_ge(s["silu"], i + 1)
                    dve.wait_ge(s["done"], unit + MSPLIT + 1)
                    dve.tensor_tensor(act_row[:, :], ps[:, 1, :], silu_g[:, :], ALU.mult).then_inc(s["act"], 1)

                def act_lo(i):
                    dve.wait_ge(s["ahi"], i + 1)
                    dve.tensor_tensor(xT_lo_all[:, 2, :], ps[:, 4, :], xT_hi_all[:, 2, :].bitcast(F), ALU.subtract
                                      ).then_inc(s["alo"], 1)

                rows_lo(0)
                m_lo(l, 3, 0)
                act_mul(0, 3)
                rows_lo(1)
                m_lo(l, 4, 0)
                m_lo(l, 5, 0)
                dve.wait_ge(routed, 2 * l + 2)
                n = later_items(dve) + 1
                with dve.Fori(1, n) as i:
                    rev = i - 1
                    act_lo(i - 1)
                    for c in range(6, 10):
                        m_lo(l, c, rev)
                    act_mul(i, i * 6 + 1)
                    rows_lo(i + 1)
                    m_lo(l, 10, rev)
                    m_lo(l, 11, rev)
                act_lo(n - 1)
                for r in range(NT):
                    dve.wait_ge(s["pick_in"][r], 32)
                    after(dve.scalar_tensor_tensor(out=h[:, r, :], in0=y_pick[2 * r][:, :], scalar=gates[:, 0, r:r + 1],
                                                   in1=h[:, r, :], op0=ALU.mult, op1=ALU.add))
                    dve.scalar_tensor_tensor(out=h[:, r, :], in0=y_pick[2 * r + 1][:, :],
                                             scalar=gates[:, 1, r:r + 1], in1=h[:, r, :], op0=ALU.mult,
                                             op1=ALU.add).then_inc(h_ready, 1)

            dve.sem_inc(split_lo, RAW)
            for l in range(2):
                dve.sem_inc(M[l]["lo"], MRAW)
            dve.wait_ge(pos_in, 16)
            dve.wait_ge(consts_ready, 1)
            after(dve.tensor_copy(pos_f[:, :], pos_i[:, :]))
            for r in range(NT):
                last = dve.tensor_scalar(ang[:, r, :], inv_f[:, :], pos_f[:, r:r + 1], None, ALU.mult)
            after(last)
            two_pi = 2 * np.pi
            p1 = 6.28125
            p2 = float(np.float32(np.floor((two_pi - p1) * 2 ** 18) / 2 ** 18))
            p3 = float(np.float32(two_pi - p1 - p2))
            for j, quarter in enumerate((0.0, 0.25)):
                after(dve.tensor_scalar(turns[:, j], ang[:, :, :], 1 / two_pi, quarter, ALU.mult, ALU.add))
                after(dve.tensor_copy(turns_i[:, j], turns[:, j]))
                after(dve.tensor_copy(turns[:, j], turns_i[:, j]))
                after(dve.scalar_tensor_tensor(out=red[:, j], in0=turns[:, j], scalar=-p1, in1=ang[:, :, :],
                                               op0=ALU.mult, op1=ALU.add))
                after(dve.scalar_tensor_tensor(out=red[:, j], in0=turns[:, j], scalar=-p2, in1=red[:, j],
                                               op0=ALU.mult, op1=ALU.add))
                after(dve.scalar_tensor_tensor(out=red[:, j], in0=turns[:, j], scalar=-p3, in1=red[:, j],
                                               op0=ALU.mult, op1=ALU.add))
                if j:
                    after(dve.tensor_scalar(red[:, j], red[:, j], float(np.pi / 2), None, ALU.add))
                ins = dve.tensor_scalar(red[:, j], red[:, j], 3.1415925, -3.1415925, ALU.min, ALU.max)
            ins.then_inc(trig_ready, 1)
            dve.wait_ge(trig_ready, 1)
            dve.wait_ge(consts_ready, 2)
            after(dve.tensor_scalar(row_m[:, :], row_i[:, :], 3, None, ALU.bitwise_and))
            after(dve.tensor_copy(row_mf[:, :], row_m[:, :]))
            after(dve.tensor_scalar(dil0[:, :, :], dil0[:, :, :], row_mf[:, :], None, ALU.is_equal))
            dve.tensor_scalar(dil[:, :, :], dil0[:, :, :], -NEG, NEG, ALU.mult, ALU.add).then_inc(rows_ready, 1)
            after(dve.tensor_scalar(row_m[:, :], row_i[:, :], 4, None, ALU.arith_shift_right))
            after(dve.tensor_copy(row_mf[:, :], row_m[:, :]))
            dve.tensor_scalar(cand_j[:, :], row_mf[:, :], float(P), -0.5, ALU.mult, ALU.add)
            dve.wait_ge(trig_done, 1)
            for half, sign in ((0, -1.0), (32, 1.0)):
                dve.tensor_copy(cos_t[:, :, half:half + 32], trig[:, 1])
                after(dve.tensor_scalar(sin_t[:, :, half:half + 32], trig[:, 0], sign, None, ALU.mult))
            router_split(0)
            norm_rows(0, 0, True)
            turn_lo(0)
            dve.wait_ge(conv_t, 1)
            after(dve.tensor_copy(conv_c[:, :], ps[:, 7, 0:24]))
            lo(0)
            lo(1)
            base_step = steps[0]
            conv_chain = 5
            with dve.Fori(0, 2) as c:
                def link(ins, k):
                    ins.then_inc(dve_step, 1)
                    dve.wait_ge(dve_step, c * (4 * conv_chain) + (base_step + k + 1))
                for q in range(3):
                    lo(2 * q + 2, c)
                    for b in range(4):
                        if q == 1:
                            k = conv_chain * b
                            wait_in_block(dve, c, 1, b)
                            dve.wait_ge(c_ready, c * 4 + b + 1)
                            uv, cv = u_pad[:, b], conv_o[:, b, :].rearrange("p (r a) -> p r a", r=NT)
                            dve.tensor_tensor(uv[:, :, 1:1 + P], ps[:, b, :].rearrange("p (r a) -> p r a", r=NT),
                                              c_gate[:, b, :].rearrange("p (r a) -> p r a", r=NT), ALU.mult
                                              ).then_inc(u_ready, 1)
                            dve.wait_ge(u_ready, c * 4 + b + 1)

                            def tap(t):
                                return conv_c[:, bass.ds(c * 4 + (8 * t + b), 1)]

                            def add(o, i, t, k):
                                link(dve.scalar_tensor_tensor(out=o, in0=i, scalar=tap(t), in1=o, op0=ALU.mult,
                                                              op1=ALU.add), k)
                            link(dve.tensor_scalar(cv, uv[:, :, 1:1 + P], tap(2), None, ALU.mult), k)
                            add(cv[:, 1:4, :], uv[:, 0:3, 1:1 + P], 1, k + 1)
                            add(cv[:, 0, :], uv[:, 3, 0:P], 1, k + 2)
                            add(cv[:, 2:4, :], uv[:, 0:2, 1:1 + P], 0, k + 3)
                            add(cv[:, 0:2, :], uv[:, 2:4, 0:P], 0, k + 4)
                        if q == 2:
                            wait_in_block(dve, c, 2, b)
                            dve.tensor_tensor(conv_o[:, b, :], ps[:, b, :], conv_o[:, b, :], ALU.mult
                                              ).then_inc(gated, 1)
                    if q == 2:
                        for b in range(4):
                            dve.wait_ge(mix_hi, c * 4 + b + 1)
                            dst = mixT_lo[:, bass.ds(c * 4 + b, 1), :].rearrange("p a n -> p (a n)")
                            src = mixT_hi[:, bass.ds(c * 4 + b, 1), :].rearrange("p a n -> p (a n)").bitcast(F)
                            dve.tensor_tensor(dst, conv_o[:, b, :], src, ALU.subtract).then_inc(mix_lo, 1)
                    lo(2 * q + 3, c)
            steps[0] = base_step + 2 * 4 * conv_chain
            lo(14)
            lo(15)
            residual_add(0, U_OUT)
            norm_rows(1, 4, True)
            turn_lo(1)
            for c in range(MSPLIT):
                m_lo(0, c, 0)
            route(0)
            experts(0)
            router_split(1)
            norm_rows(2, 8, True)
            turn_lo(2)
            dve.sem_inc(masked, 2)
            lo(U_QKV)
            lo(U_QKV + 1)

            def mask_scores(w, s32):
                r = w % NT
                b = 2 * (w % 2)
                dve.wait_ge(scored, s32 + w + 1)
                dve.wait_ge(p_turned, s32 + w + 1)
                dve.sem_inc(dve_passed, 1)
                dve.tensor_tensor_reduce(out=prob[w % 2][:, :],
                                         in0=ps[:, b:b + 2, :].rearrange("p a n -> p (a n)")[:, 0:KEYS],
                                         in1=mask[:, r, :], scale=-SCALE, scalar=3e38, op0=ALU.add, op1=ALU.min,
                                         accum_out=neg_max[:, w:w + 1]).then_inc(masked, 1)

            def scale_probs(w, s32):
                dve.wait_ge(expd, s32 + w + 1)
                dve.reciprocal(inv_den[:, w:w + 1], denom[:, w:w + 1]).then_inc(inverted, 1)
                dve.wait_ge(inverted, s32 + w + 1)
                dve.tensor_scalar(prob[w % 2][:, :], prob[w % 2][:, :], inv_den[:, w:w + 1], None, ALU.mult
                                  ).then_inc(scaled, 1)

            with dve.Fori(0, 2) as s:
                with dve.Fori(0, NATT) as g:
                    for p in range(3):
                        rev = s * 3 + g
                        lo(U_QKV + 2 * p + 2, rev)
                        if p < 2:
                            g4 = (s * 6 + g * 2 + p) * 4
                            for r in range(NT):
                                wait_qkv(dve, rev, p, r)
                                dve.wait_ge(rope_added, g4 + r + 1)
                                t = ps[:, r, :].rearrange("p (h d) -> p h d", d=HD)
                                av = rope_a[r % 2][:, :].rearrange("p (h d) -> p h d", d=HD)
                                bv = rope_b[r % 2][:, :].rearrange("p (h d) -> p h d", d=HD)
                                cb = cos_t[:, r, :].unsqueeze(1).to_broadcast([P, 8, HD])
                                dve.tensor_tensor(av, t, cb, ALU.mult)
                                for x0, x1 in ((0, 32), (32, 0)):
                                    sb_ = sin_t[:, r, x0:x0 + 32].unsqueeze(1).to_broadcast([P, 8, 32])
                                    ins = dve.tensor_tensor(bv[:, :, x0:x0 + 32], t[:, :, x1:x1 + 32], sb_, ALU.mult)
                                ins.then_inc(rope_in, 1)
                        lo(U_QKV + 2 * p + 3, rev)
                s32 = s * 32
                mask_scores(0, s32)
                scale_probs(0, s32)
                for w in range(32):
                    if w + 1 < 32:
                        mask_scores(w + 1, s32)
                    dve.wait_ge(p_turned, s32 + w + 1 + 2)
                    dve.tensor_copy(probT[:, 512:KEYS], ps[:, 5, 0:256]).then_inc(pt_b, 1)
                    if w + 1 < 32:
                        scale_probs(w + 1, s32)
            for j in range(4):
                dve.wait_ge(x_hi, 12 + j + 1)
                dve.tensor_tensor(xT_lo_all[:, 2 * j:2 * j + 2, :].rearrange("p a n -> p (a n)"), out_blocks(j),
                                  xT_hi_all[:, 2 * j:2 * j + 2, :].rearrange("p a n -> p (a n)").bitcast(F),
                                  ALU.subtract).then_inc(x_lo, 1)
            lo(54)
            lo(55)
            dve.wait_ge(h_back, 16)
            residual_add(1, U_O)
            norm_rows(3, 12, True)
            turn_lo(4)
            for c in range(MSPLIT):
                m_lo(1, c, 0)
            route(1)
            experts(1)
            norm_rows(4, 16, False)

        @block.tensor
        def _(pe):
            def turn_rows(stage, first):
                for r in range(NT):
                    b = 2 * (r % 2)
                    pe.wait_ge(hn_ready, first + r + 1)
                    if r >= 2:
                        pe.wait_ge(x_lo, 4 * stage + r - 1)
                    for k in range(KD):
                        rows = hn[r % 2][:, k * P:(k + 1) * P]
                        ins = pe.transpose(ps[:, b + k // 4, (k % 4) * P:(k % 4 + 1) * P], rows, ident[:, :])
                    ins.then_inc(x_turned, 1)

            def project(u0, xh, xl):
                for c in range(2):
                    for kh in range(2):
                        u = u0 + 2 * c + kh
                        pe.wait_ge(split_lo, RAW + u + 1)
                        for r in range(NT):
                            for k in range(4):
                                ins = product(pe, ps[:, 4 * c + r, :], xh[:, 4 * kh + k, r * P:(r + 1) * P],
                                              xl[:, 4 * kh + k, r * P:(r + 1) * P], W_hi[u % 2][:, k, :],
                                              W_lo[u % 2][:, k, :], kh == 0 and k == 0, kh == 1 and k == 3)
                            if kh == 1 and r < NT - 1:
                                ins.then_inc(proj_done, 1)
                        ins.then_inc(unit_done, 1)

            def router(l):
                pe.wait_ge(wr_ready, l + 1)
                pe.wait_ge(x_lo, (4 if l == 0 else 16) + 4)
                for r in range(NT):
                    for k in range(KD):
                        ins = product(pe, ps[:, 4, 20 * r:20 * r + 20], xT_hi_all[:, k, r * P:(r + 1) * P],
                                      xT_lo_all[:, k, r * P:(r + 1) * P], wr_hi[:, k, :], wr_lo[:, k, :],
                                      k == 0, k == KD - 1)
                ins.then_inc(logits_done, 1)
                pe.wait_ge(used_ready, 2 * l + 1)
                for r in range(NT):
                    for q in range(r + 1):
                        ins = pe.matmul(ps[:, 5, 16 * r:16 * r + 16], (ones if q < r else below)[:, :],
                                        used[:, q, :], start=(q == 0), stop=(q == r))
                pe.wait_ge(used_ready, 2 * l + 2)
                pe.matmul(ps[0:CAND, 6, 0:1], row_counts[:, :, :].rearrange("p j e -> p (j e)"), ones[:, 0:1],
                          start=True, stop=True).then_inc(pos_done, 1)
                for n in range(8):
                    pe.wait_ge(onehots, 8 * l + n + 1)
                    ins = pe.matmul(ps[:, 5, 128:128 + CAND], lane_oh[n % 2][:, :], blk_oh[n % 2][:, :],
                                    start=(n == 0), stop=(n == 7))
                    ins.then_inc(list_step, 1)
                pe.wait_ge(valid_ready, l + 1)
                pe.matmul(ps[0:CAND, 7, 0:1], below[0:CAND, 0:CAND], valid[0:CAND, :], start=True, stop=True
                          ).then_inc(rank_done, 1)
                pe.wait_ge(item_oh_ready, l + 1)
                pe.matmul(ps[0:1, 6, 64:64 + ITEM_COLS], cand_c[0:CAND, :], item_oh[:, 0:ITEM_COLS], start=True,
                          stop=True)
                pe.matmul(ps[0:1, 6, 64 + ITEM_COLS:65 + ITEM_COLS], valid[0:CAND, :], ones[0:CAND, 0:1], start=True,
                          stop=True).then_inc(items_done, 1)

            def experts(l):
                s = M[l]
                xh = xT_hi_all[:, 0:2, :].rearrange("p a (k n) -> p (a k) n", n=P)
                xl = xT_lo_all[:, 0:2, :].rearrange("p a (k n) -> p (a k) n", n=P)
                ah, al = (t[:, 2, :].rearrange("p (k n) -> p k n", n=P) for t in (xT_hi_all, xT_lo_all))

                def turn_x(i):
                    pe.wait_ge(s["rows_in"], i * 16 + 16)
                    for k in range(KD):
                        ins = pe.transpose(ps[:, 2 + k // 4, (k % 4) * P:(k % 4 + 1) * P],
                                           x_rows[:, k * P:(k + 1) * P], ident[:, :])
                    ins.then_inc(s["turned"], 1)

                def turn_act(i):
                    pe.wait_ge(s["act"], i + 1)
                    for k in range(KF):
                        ins = pe.transpose(ps[:, 4, k * P:(k + 1) * P], act_row[:, k * P:(k + 1) * P], ident[:, :])
                    ins.then_inc(s["aturned"], 1)

                def up_unit(c, i6, j):
                    b = c % MSPLIT
                    pe.wait_ge(s["lo"], i6 + c + 1 + MRAW)
                    for k in range(4):
                        ins = product(pe, ps[:, j // 2, :], xh[:, 4 * (j % 2) + k, :], xl[:, 4 * (j % 2) + k, :],
                                      MW_hi[b][:, k, :], MW_lo[b][:, k, :], j % 2 == 0 and k == 0,
                                      j % 2 == 1 and k == 3)
                    ins.then_inc(s["done"], 1)

                def down_unit(c, i6, j):
                    b = c % MSPLIT
                    pe.wait_ge(s["lo"], i6 + c + 1 + MRAW)
                    for k in range(2):
                        for half in range(2):
                            ins = product(pe, ps[:, 5 + half, :], ah[:, 2 * j + k, :], al[:, 2 * j + k, :],
                                          MW_hi[b][:, 2 * k + half, :], MW_lo[b][:, 2 * k + half, :],
                                          j == 0 and k == 0, j == 1 and k == 1)
                    ins.then_inc(s["done"], 1)

                turn_x(0)
                pe.wait_ge(s["xlo"], 1)
                for j in range(4):
                    up_unit(j, 0, j)
                turn_x(1)
                pe.wait_ge(routed, 2 * l + 2)
                n = later_items(pe) + 1
                with pe.Fori(1, n) as i:
                    i6 = i * 6 - 6
                    pe.wait_ge(s["xlo"], i + 1)
                    pe.wait_ge(s["act"], i)
                    up_unit(4, i6, 0)
                    turn_act(i - 1)
                    for j in range(1, 4):
                        up_unit(4 + j, i6, j)
                    turn_x(i + 1)
                    pe.wait_ge(s["alo"], i)
                    pe.wait_ge(s["y"], i)
                    down_unit(8, i6, 0)
                    down_unit(9, i6, 1)
                turn_act(n - 1)
                pe.wait_ge(s["alo"], n)
                pe.wait_ge(s["y"], n)
                down_unit(4, n * 6 - 6, 0)
                down_unit(5, n * 6 - 6, 1)

            pe.sem_inc(unit_done, SPLIT)
            pe.sem_inc(gated, 4)
            for l in range(2):
                pe.sem_inc(M[l]["done"], MSPLIT)
                pe.sem_inc(M[l]["y"], 1)
            pe.wait_ge(consts_ready, 1)
            pe.wait_ge(conv_in, 16)
            pe.transpose(ps[:, 7, 0:24], conv_rows[:, :], ident[0:24, 0:24]).then_inc(conv_t, 1)
            turn_rows(0, 0)
            pe.wait_ge(x_lo, 4)
            with pe.Fori(0, 2) as c:
                for q in range(3):
                    for kh in range(2):
                        uc = 2 * q + kh
                        pe.wait_ge(split_lo, c * 6 + RAW + uc + 1)
                        for b in range(4):
                            if kh == 0:
                                pe.wait_ge((gated, c_ready, u_ready)[q], c * 4 + b + 1)
                            for k in range(4):
                                ws = slice(b * P, (b + 1) * P)
                                ins = product(pe, ps[:, b, :], W_hi[uc % 2][:, k, ws], W_lo[uc % 2][:, k, ws],
                                              xT_hi_all[:, 4 * kh + k, :], xT_lo_all[:, 4 * kh + k, :],
                                              kh == 0 and k == 0, kh == 1 and k == 3)
                            if kh == 1 and b < 3:
                                ins.then_inc(block_done, 1)
                        ins.then_inc(unit_done, 1)
            pe.wait_ge(mix_lo, 8)
            project(U_OUT, mixT_hi, mixT_lo)
            turn_rows(1, 4)
            router(0)
            experts(0)
            turn_rows(2, 8)
            pe.wait_ge(x_lo, 12)
            pe.sem_inc(v_ready, 4)
            pe.sem_inc(rope_added, 2)
            pe.sem_inc(qk_turned, 4)
            pe.sem_inc(p_turned, 2)
            pe.sem_inc(pt_a, 1)
            pe.sem_inc(pt_b, 1)
            pe.sem_inc(o_stored, 1)
            pe.sem_inc(qkT_ready, 2)
            pe.wait_ge(consts_ready, 3)

            with pe.Fori(0, 2) as s:
                with pe.Fori(0, NATT) as g:
                    for p in range(3):
                        for kh in range(2):
                            uc, ui = U_QKV + 2 * p + kh, s * 18 + g * 6
                            pe.wait_ge(split_lo, ui + RAW + uc + 1)
                            for r in range(NT):
                                if kh == 0 and p == 0:
                                    pe.wait_ge(v_ready, (s * 3 + g) * 4 + r + 1)
                                elif kh == 0:
                                    pe.wait_ge(rope_in, (s * 6 + g * 2 + p - 1) * 4 + r + 1)
                                for k in range(4):
                                    ins = product(pe, ps[:, r, :], xT_hi_all[:, 4 * kh + k, r * P:(r + 1) * P],
                                                  xT_lo_all[:, 4 * kh + k, r * P:(r + 1) * P],
                                                  W_hi[uc % 2][:, k, :], W_lo[uc % 2][:, k, :],
                                                  kh == 0 and k == 0, kh == 1 and k == 3)
                                if kh == 1 and r < NT - 1:
                                    ins.then_inc(qkv_done, 1)
                            ins.then_inc(unit_done, 1)
                            if kh == 0 and p > 0:
                                g4 = (s * 6 + g * 2 + p - 1) * 4
                                for r in range(NT):
                                    pe.wait_ge(rope_added, g4 + r + 1 + 2)
                                    pe.wait_ge(qkT_ready, g4 + r + 1)
                                    for hb in range(4):
                                        tr = pe.transpose(ps[:, 4 + r % 2, hb * P:(hb + 1) * P],
                                                          qk_rot[:, r, hb * P:(hb + 1) * P], ident[:, :])
                                    tr.then_inc(qk_turned, 1)
                s32 = s * 32
                pe.wait_ge(qkT_ready, s * 24 + 24 + 2)
                pe.wait_ge(v_ready, s * 12 + 12 + 4)

                def scores(w):
                    head, r = w // NT, w % NT
                    q, hb, b = q_pad[head % 2], head // 2, 2 * (w % 2)
                    if r == 0:
                        pe.wait_ge(q_padded, s * 8 + head + 1)
                    pe.wait_ge(masked, s32 + w + 1)
                    tile_r = slice(r * P, (r + 1) * P)
                    pe.matmul(ps[:, b, :], q[:, 0, tile_r], qkT[:, 0, 1, hb, :], start=True, stop=True)
                    pe.matmul(ps[:, b + 1, 0:P], q[:, 1, tile_r], qkT[:, 1, 1, hb, tile_r], start=True, stop=True)
                    pe.matmul(ps[:, b + 1, P:2 * P], q[:, 2, tile_r], qkT[:, 2, 1, hb, tile_r],
                              start=True, stop=True).then_inc(scored, 1)

                def weighted(w):
                    head, r = w // NT, w % NT
                    o = ps[HD * (head % 2):HD * (head % 2) + HD, 6, r * P:(r + 1) * P]
                    cols = slice(head * HD, head * HD + HD)
                    if w % 8 == 0:
                        pe.wait_ge(o_stored, s * 4 + w // 8 + 1)
                    pe.wait_ge(pt_a, s32 + w + 2)
                    pe.wait_ge(pt_b, s32 + w + 2)
                    keys = [(0, q) for q in range(NT)] + [(1, r), (2, r)]
                    for n, (g, q) in enumerate(keys):
                        ins = pe.matmul(o, v_all[:, g, q, cols], probT[:, n * P:(n + 1) * P], start=(n == 0),
                                        stop=(n == 5))
                    ins.then_inc(pv_done, 1)

                scores(0)
                for w in range(32):
                    if w + 1 < 32:
                        scores(w + 1)
                    if w:
                        weighted(w - 1)
                    pe.wait_ge(scaled, s32 + w + 1)
                    pe.wait_ge(pt_a, s32 + w + 1)
                    pe.wait_ge(pt_b, s32 + w + 1)
                    for n in range(6):
                        ins = pe.transpose(ps[:, 4 + n // 4, (n % 4) * P:(n % 4 + 1) * P],
                                           prob[w % 2][:, n * P:(n + 1) * P], ident[:, :])
                    ins.then_inc(p_turned, 1)
                weighted(31)
            pe.wait_ge(x_lo, 16)
            project(U_O, xT_hi_all, xT_lo_all)
            turn_rows(4, 12)
            router(1)
            experts(1)


_INS = ["x", "positions", "norm_mix", "norm_ffn", "norm_final", "conv_w_in", "conv_w", "conv_w_out", "attn_w_qkv",
        "attn_w_o", "w_coarse", "b_coarse", "w_fine", "b_fine", "w_gate", "w_up", "w_down"]


def kernel(**inputs):
    import concourse.bacc as bacc
    from concourse.bass_utils import run_bass_kernel_spmd

    nc = bacc.Bacc("TRN2", target_bir_lowering=False, num_devices=1)
    arrays, args = {}, []
    for name in _INS:
        a = np.ascontiguousarray(inputs[name])
        arrays[f"in_{name}_dram"] = a
        args.append(nc.dram_tensor(f"in_{name}_dram", a.shape, mybir.dt.from_np(a.dtype), kind="ExternalInput").ap())
    out = nc.dram_tensor("out_0_dram", (1, S, D), F, kind="ExternalOutput").ap()
    build(nc, *args, out)
    r = run_bass_kernel_spmd(nc, [arrays], core_ids=[0])
    return r.results[0]["out_0_dram"]
```

```python
from contextlib import ExitStack

import numpy as np

import concourse.bass as bass
from concourse import mybir

ALU = mybir.AluOpType
ACT = mybir.ActivationFunctionType
AX = mybir.AxisListType
F = mybir.dt.float32
FR = mybir.dt.float32r
BF = mybir.dt.bfloat16
I32 = mybir.dt.int32

P = 128
D = 1024
S = 512
NT = S // P
KD = D // P
FF = 512
KF = FF // P
NG, NPG = 4, 4
NE = NG * NPG
HD = 64
NATT = 3
KB = 1024
EPS = 1e-6
NEG = -1e30
CAND = NE * NT
MAX_ITEMS = NE + 2 * S // P
MIN_ITEMS = NE
ITEM_COLS = 32
KEYS = S + 2 * P
SCALE = HD ** -0.5
ROPE_THETA = 10000.0
RAW, SPLIT = 3, 2
MRAW, MSPLIT = 6, 3
U_OUT, U_QKV, U_O, U_END = 12, 16, 52, 56


def build(nc, x, positions, norm_mix, norm_ffn, norm_final, conv_w_in, conv_w, conv_w_out, attn_w_qkv,
          attn_w_o, w_coarse, b_coarse, w_fine, b_fine, w_gate, w_up, w_down, out):
    hn_dram = nc.dram_tensor("hn_rows", (S, D), F, kind="Internal").ap()
    y_dram = nc.dram_tensor("y_rows", (2 * S, D), F, kind="Internal").ap()
    h_dram = nc.dram_tensor("h_rows", (NT, P, D), F, kind="Internal").ap()

    x_v = x.rearrange("b (a r) d -> (b a) r d", r=NT)
    out_v = out.rearrange("b (a r) d -> (b a) r d", r=NT)
    pos_v = positions.rearrange("b (a r) -> (b a) r", r=NT)
    gains = [norm_mix[0:1, :], norm_ffn[0:1, :], norm_mix[1:2, :], norm_ffn[1:2, :],
             norm_final.rearrange("(o d) -> o d", o=1)]
    w_in_v = conv_w_in.rearrange("l (p k) n -> (l p) k n", k=KD)
    w_qkv_v = attn_w_qkv.rearrange("l (p k) n -> (l p) k n", k=KD)
    w_out_v = conv_w_out.rearrange("l (k p) n -> (l p) k n", p=P)
    w_o_v = attn_w_o.rearrange("l (k p) n -> (l p) k n", p=P)
    gate_v = w_gate.rearrange("l e (p k) n -> l e p k n", k=KD)
    up_v = w_up.rearrange("l e (p k) n -> l e p k n", k=KD)
    down_v = w_down.rearrange("l e (k p) n -> l e p k n", p=P)

    with ExitStack() as ctx:
        base = -(-nc.sbuf_base // 64) * 64

        def at(name, shape, dt, off):
            return nc.alloc_sbuf_tensor_at(name, shape, dt, offset=base + int(off))

        A, B = 0, 16 * KB
        C = B + 32 * KB
        DR = C + 32 * KB
        E = DR + 24 * KB
        FG = E + int(72.25 * KB)
        G = FG + 16 * KB
        h = at("h", [P, NT, D], F, A)
        oT = at("oT", [P, 12 * D], F, A)
        O_HALF = 10 * D
        xT_hi_all = at("xT_hi_all", [P, KD, S], FR, B)
        xT_lo_all = at("xT_lo_all", [P, KD, S], FR, B + 16 * KB)
        W_hi = [at(f"W_hi{i}", [P, 4, 512], FR, C + 16 * KB * i) for i in range(2)]
        W_lo = [at(f"W_lo{i}", [P, 4, 512], FR, C + 16 * KB * i + 8 * KB) for i in range(2)]
        raw = [at(f"raw{i}", [P, 4, 512], F, DR + 8 * KB * i) for i in range(RAW)]
        c_gate = at("c_gate", [P, 4, 512], F, E)
        conv_o = at("conv_o", [P, 4, 512], F, E + 8 * KB)
        u_pad = at("u_pad", [P, 4, NT, 1 + P], F, E + 16 * KB)
        mixT_hi = at("mixT_hi", [P, KD, S], FR, E + int(24.25 * KB))
        mixT_lo = at("mixT_lo", [P, KD, S], FR, E + int(40.25 * KB))
        m_off = [0, 8, 16, 56.25, 64.25, 24.25]
        m_raw = [at(f"m_raw{i}", [P, 4, 512], F, E + int(o * KB)) for i, o in enumerate(m_off)]
        MW_hi = W_hi + [at("W_hi2", [P, 4, 512], FR, E + int(32.25 * KB))]
        MW_lo = W_lo + [at("W_lo2", [P, 4, 512], FR, E + int(40.25 * KB))]
        x_rows = at("x_rows", [P, D], F, E + int(48.25 * KB))
        y_rows = at("y_rows_sb", [P, D], F, E + int(52.25 * KB))
        y_pick = [at(f"y_pick{i}", [P, D], F, E + int((4 * i if i < 6 else 56.25 + 4 * (i - 6)) * KB))
                  for i in range(2 * NT)]
        qkT = at("qkT", [P, NATT, 2, 4, S], F, E)
        v_all = at("v_all", [P, NATT, NT, 512], F, E + 48 * KB)
        hn = [at(f"hn{i}", [P, D], F, FG + 4 * KB * i) for i in range(2)]
        gain = at("gain", [P, D], F, FG + 8 * KB)
        square_out = at("square_out", [P, D], F, FG + 12 * KB)
        silu_g = at("silu_g", [P, FF], F, FG + 12 * KB)
        act_row = at("act_row", [P, FF], F, FG + 14 * KB)
        qk_rot = at("qk_rot", [P, NT, 512], F, FG)
        rope_a = [at(f"rope_a{i}", [P, 512], F, FG + 8 * KB + 2 * KB * i) for i in range(2)]
        rope_b = [at(f"rope_b{i}", [P, 512], F, FG + 12 * KB + 2 * KB * i) for i in range(2)]
        prob = [at(f"prob{i}", [P, KEYS], F, FG + 3 * KB * i) for i in range(2)]
        probT = at("probT", [P, KEYS], F, FG + 6 * KB)
        q_pad = [at("q_pad0", [P, NATT, S], F, A + 8 * KB), at("q_pad1", [P, NATT, S], F, FG + 9 * KB)]
        rt_off = [E + int(52.25 * KB)]

        def temp(name, shape, dt=F):
            n = 4 * int(np.prod(shape[1:]))
            t = at(name, shape, dt, rt_off[0])
            rt_off[0] += -(-n // 32) * 32
            assert rt_off[0] <= E + int(56.25 * KB)
            return t

        g_off = [G]

        def keep(name, shape, dt=F):
            n = (2 if dt == BF else 4) * int(np.prod(shape[1:]))
            t = at(name, shape, dt, g_off[0])
            g_off[0] += -(-n // 32) * 32
            return t

        ident = keep("ident", [P, P])
        below = keep("below", [P, P])
        ones = keep("ones", [P, P])
        iota_f = keep("iota_f", [P, P])
        mask = keep("mask", [P, NT, KEYS], BF)
        cos_t = keep("cos_t", [P, NT, HD])
        sin_t = keep("sin_t", [P, NT, HD])
        conv_rows = keep("conv_rows", [24, P])
        conv_c = keep("conv_c", [P, 24])
        wc_raw = keep("wc_raw", [P, KD, NG])
        wf_raw = keep("wf_raw", [P, NG, KD, NPG])
        wr2 = keep("wr2", [P, KD, 40], FR)
        wr = keep("wr", [P, KD, 20])
        bias_r = keep("bias_r", [P, 20])
        ssq = keep("ssq", [P, NT])
        msq = keep("msq", [P, NT])
        rstd = keep("rstd", [P, NT])
        neghalf = keep("neghalf", [P, 1])
        neg_max = keep("neg_max", [P, 32])
        denom = keep("denom", [P, 32])
        inv_den = keep("inv_den", [P, 32])
        gates = keep("gates", [P, 2, NT])
        dest_list = keep("dest_list", [P, CAND], I32)
        tok_list = keep("tok_list", [P, CAND], I32)
        tok_col = keep("tok_col", [P, 1], I32)
        dest_col = keep("dest_col", [P, 1], I32)
        items = keep("items", [1, ITEM_COLS + 2], I32)
        dest_id = keep("dest_id", [P, 2, NT])
        cand_j = keep("cand_j", [P, 1])
        cand_c = keep("cand_c", [P, 1])
        rank4 = keep("rank4", [P, 4])
        exp512 = keep("exp512", [P, NE])
        assert base + g_off[0] <= nc.sbuf_usable_end, (base + g_off[0], nc.sbuf_usable_end)
        s_off = [E + int(56.25 * KB)]

        def start_temp(name, shape, dt=F):
            t = at(name, shape, dt, s_off[0])
            s_off[0] += -(-4 * int(np.prod(shape[1:])) // 32) * 32
            return t

        pos_i = start_temp("pos_i", [P, NT], I32)
        pos_f = start_temp("pos_f", [P, NT])
        inv_f = start_temp("inv_f", [P, 32])
        ang = start_temp("ang", [P, NT, 32])
        turns = start_temp("turns", [P, 2, NT, 32])
        turns_i = start_temp("turns_i", [P, 2, NT, 32], I32)
        red = start_temp("red", [P, 2, NT, 32])
        trig = start_temp("trig", [P, 2, NT, 32])
        row_i = start_temp("row_i", [P, 1], I32)
        row_m = start_temp("row_m", [P, 1], I32)
        row_mf = start_temp("row_mf", [P, 1])
        dil = start_temp("dil", [P, 32, 4])
        dil0 = start_temp("dil0", [P, 32, 4])
        lgT = at("lgT", [40, S], F, FG + 12 * KB)
        lg = temp("lg", [P, NT, 20])
        m1 = temp("m1", [P, NT])
        m2 = temp("m2", [P, NT])
        t4 = temp("t4", [P, NT, NG])
        oh_g = temp("oh_g", [P, NT, NG])
        t16 = temp("t16", [P, NT, NG, NPG])
        fsel = temp("fsel", [P, NT, NPG])
        o1 = temp("o1", [P, NT, NPG])
        o2 = temp("o2", [P, NT, NPG])
        e1 = temp("e1", [P, NT, NG, NPG])
        e2 = temp("e2", [P, NT, NG, NPG])
        used = temp("used", [P, NT, NE])
        row_count = temp("row_count", [P, NE])
        row_counts = temp("row_counts", [P, NT, NE])
        ptop = temp("ptop", [P, NT])
        ex = temp("ex", [P, NT])
        rs = temp("rs", [P, NT])
        slot_f = temp("slot_f", [P, 2, NT])
        slot_i = temp("slot_i", [P, 2, NT], I32)
        lane_i = temp("lane_i", [P, 2, NT], I32)
        blk_i = temp("blk_i", [P, 2, NT], I32)
        exp_i = temp("exp_i", [P, 2, NT], I32)
        lane_f = temp("lane_f", [P, 2, NT])
        cand_f = temp("cand_f", [P, 2, NT])
        lane_oh = [at(f"lane_oh{i}", [P, P], FR, FG + 14 * KB + 512 * i) for i in range(2)]
        blk_oh = [temp(f"blk_oh{i}", [P, CAND], FR) for i in range(2)]
        valid = temp("valid", [P, 1])
        item_oh = temp("item_oh", [CAND, ITEM_COLS + 1])
        item_v = temp("item_v", [CAND, 1])

        ps = ctx.enter_context(nc.psum_tensor("ps", [P, 8, 512], F))

        def sem(name):
            return ctx.enter_context(nc.semaphore(name))

        gain_in = sem("gain_in")
        x_in = [sem(f"x_in{r}") for r in range(NT)]
        sp_passed, pool_passed, dve_passed = sem("sp_passed"), sem("pool_passed"), sem("dve_passed")
        pos_in, conv_in = sem("pos_in"), sem("conv_in")
        router_in = sem("router_in")
        raw_in = [sem(f"raw_in{i}") for i in range(RAW)]
        split_hi, split_lo, unit_done = sem("split_hi"), sem("split_lo"), sem("unit_done")
        pool_step, dve_step, act_step = sem("pool_step"), sem("dve_step"), sem("act_step")
        consts_ready, rows_ready, trig_ready, trig_done = (
            sem("consts_ready"), sem("rows_ready"), sem("trig_ready"), sem("trig_done"))
        conv_t, conv_taps = sem("conv_t"), sem("conv_taps")
        ssq_ready, rstd_ready, hn_ready, h_ready = sem("ssq_ready"), sem("rstd_ready"), sem("hn_ready"), sem("h_ready")
        x_turned, x_hi, x_lo = sem("x_turned"), sem("x_hi"), sem("x_lo")
        block_done, u_ready = sem("block_done"), sem("u_ready")
        gated, mix_hi, mix_lo = sem("gated"), sem("mix_hi"), sem("mix_lo")
        c_ready = sem("c_ready")
        proj_done = sem("proj_done")
        h_saved, h_back, qkv_done = sem("h_saved"), sem("h_back"), sem("qkv_done")
        hn_stored = [sem(f"hn_stored{i}") for i in range(2)]
        out_stored = [sem(f"out_stored{i}") for i in range(2)]
        rope_in, rope_added, qk_turned, qkT_ready, v_ready = (
            sem("rope_in"), sem("rope_added"), sem("qk_turned"), sem("qkT_ready"), sem("v_ready"))
        pads_cleared = sem("pads_cleared")
        q_padded, inverted, scaled = sem("q_padded"), sem("inverted"), sem("scaled")
        scored, masked, expd, p_turned, pt_a, pt_b, pv_done, o_stored = (
            sem("scored"), sem("masked"), sem("expd"), sem("p_turned"), sem("pt_a"), sem("pt_b"),
            sem("pv_done"), sem("o_stored"))
        logits_copied, logits_turned = sem("logits_copied"), sem("logits_turned")
        wr_ready, logits_done, ex_in, ex_out, used_ready = (
            sem("wr_ready"), sem("logits_done"), sem("ex_in"), sem("ex_out"), sem("used_ready"))
        pos_done, onehots, list_step, valid_ready, rank_done, item_oh_ready, items_done = (
            sem("pos_done"), sem("onehots"), sem("list_step"), sem("valid_ready"),
            sem("rank_done"), sem("item_oh_ready"), sem("items_done"))
        routed = sem("routed")
        M = []
        for l in range(2):
            M.append({k: sem(f"m{l}_{k}") for k in (
                "hi", "lo", "done", "rows_in", "turned", "xhi", "xlo", "silu", "act", "aturned", "ahi",
                "alo", "y", "ystored", "col", "dest", "cleared")})
            M[l]["raw_in"] = [sem(f"m{l}_raw_in{i}") for i in range(MRAW)]
            M[l]["pick_in"] = [sem(f"m{l}_pick_in{i}") for i in range(NT)]

        block = ctx.enter_context(nc.Block())

        def product(pe, o, a_hi, a_lo, b_hi, b_lo, first, last):
            pe.matmul(o, a_hi, b_hi, start=first, stop=False)
            pe.matmul(o, a_hi, b_lo, start=False, stop=False)
            return pe.matmul(o, a_lo, b_hi, start=False, stop=last)

        def wait_in_block(eng, c, q, b):
            if b < 3:
                eng.wait_ge(block_done, c * 9 + 3 * q + b + 1)
            else:
                eng.wait_ge(unit_done, c * 6 + SPLIT + 2 * q + 2)

        def wait_qkv(eng, rev, p, r):
            if r < 3:
                eng.wait_ge(qkv_done, rev * 9 + 3 * p + r + 1)
            else:
                eng.wait_ge(unit_done, rev * 6 + SPLIT + U_QKV + 2 * p + 2)

        def out_blocks(j):
            at_ = (j // 2) * O_HALF + (j % 2) * 2 * S
            return oT[:, at_:at_ + 2 * S]

        def later_items(eng):
            return eng.value_load(items[0:1, ITEM_COLS:ITEM_COLS + 1], min_val=MIN_ITEMS - 1, max_val=MAX_ITEMS - 1)

        @block.sync
        def _(sp):
            def dense(uc, rev, src):
                sp.wait_ge(split_lo, rev * 6 + uc + 1)
                sp.sem_inc(sp_passed, 1)
                sp.dma_start(raw[uc % RAW][:, :, :], src).then_inc(raw_in[uc % RAW], 16)

            def unit(l, c, rev, src, view):
                s = M[l]
                sp.wait_ge(s["lo"], rev * 6 + c + 1)
                sp.sem_inc(sp_passed, 1)
                dst = m_raw[c % MRAW][:, :, :]
                if view:
                    dst = dst.rearrange("p a n -> p (a n)").rearrange("p (k n) -> p k n", k=2)
                sp.dma_start(dst, src).then_inc(s["raw_in"][c % MRAW], 16)

            def gate_up(l, e, c, rev):
                for j in range(4):
                    w = (gate_v if j < 2 else up_v)[l, bass.ds(e, 1)].rearrange("e p k n -> (e p) k n")
                    unit(l, c + j, rev, w[:, 4 * (j % 2):4 * (j % 2) + 4, :], False)

            def down(l, e, c, rev):
                for j in range(2):
                    w = down_v[l, bass.ds(e, 1)].rearrange("e p k n -> (e p) k n")
                    unit(l, c + j, rev, w[:, 2 * j:2 * j + 2, :], True)

            def later_weights(l):
                with sp.Fori(0, NE - 2) as i:
                    gate_up(l, i + 1, 4, i)
                    down(l, i, 8, i)
                sp.wait_ge(routed, 2 * l + 2)

                def expert(i):
                    return sp.value_load(items[0:1, bass.ds(i, 1)], min_val=0, max_val=CAND - 1) % NE

                later = later_items(sp)
                with sp.Fori(NE - 2, later) as i:
                    gate_up(l, expert(i + 1), 4, i)
                    down(l, expert(i), 8, i)
                down(l, expert(later), 4, later)

            def y_back(l):
                later = later_items(sp)
                sp.wait_ge(M[l]["ystored"], later * 16 + 16)
                sp.sem_inc(sp_passed, 1)
                for r in range(NT):
                    for c in range(2):
                        sp.dma_start(y_pick[2 * r + c][:, :], y_dram[c * S + r * P:c * S + (r + 1) * P, :]
                                     ).then_inc(M[l]["pick_in"][r], 16)

            def qkv_unit(j, rev, chunk):
                col = (chunk % NATT) * (3 * D) + (chunk // NATT) * 512 + (j % 6 // 2) * D
                dense(U_QKV + j, rev, w_qkv_v[:, 4 * (j % 2):4 * (j % 2) + 4, bass.ds(col, 512)])

            def norm_gain(k):
                sp.dma_start(gain[:, :], gains[k].to_broadcast([P, D])).then_inc(gain_in, 16)

            def router_weights(l):
                sp.dma_start(wc_raw[:, :, :], w_coarse[l].rearrange("(p k) g -> p k g", k=KD)).then_inc(router_in, 16)
                for g in range(NG):
                    sp.dma_start(wf_raw[:, g, :, :], w_fine[l, g].rearrange("(p k) e -> p k e", k=KD)
                                 ).then_inc(router_in, 16)
                sp.dma_start(bias_r[:, 0:NG], b_coarse[l:l + 1, :].to_broadcast([P, NG])).then_inc(router_in, 16)
                sp.dma_start(bias_r[:, NG:NG + NE], b_fine[l].rearrange("(o g) e -> o (g e)", o=1)
                             .to_broadcast([P, NE])).then_inc(router_in, 16)

            for r in range(NT):
                sp.dma_start(h[:, r, :], x_v[:, r, :]).then_inc(x_in[r], 16)
                if r == 0:
                    norm_gain(0)
            sp.dma_start(pos_i[:, :], pos_v).then_inc(pos_in, 16)
            sp.dma_start(conv_rows[:, :], conv_w.rearrange("l t (j p) -> (l t j) p", p=P)).then_inc(conv_in, 16)
            router_weights(0)
            with sp.Fori(0, 2) as c:
                for q, col in enumerate((D, 2 * D, 0)):
                    for kh in range(2):
                        dense(2 * q + kh, c, w_in_v[:, 4 * kh:4 * kh + 4, bass.ds(c * 512 + col, 512)])
            sp.wait_ge(hn_ready, 4)
            norm_gain(1)
            for j in range(4):
                dense(U_OUT + j, 0, w_out_v[:, 4 * (j % 2):4 * (j % 2) + 4, 512 * (j // 2):512 * (j // 2) + 512])

            def store_rows(first):
                for r in range(NT):
                    sp.wait_ge(hn_ready, first + r + 1)
                    sp.dma_start(hn_dram[r * P:(r + 1) * P, :], hn[r % 2][:, :]).then_inc(hn_stored[r % 2], 16)

            sp.wait_ge(mix_lo, 8)
            sp.wait_ge(consts_ready, 3)
            gate_up(0, 0, 0, 0)
            store_rows(4)
            norm_gain(2)
            for j in range(3):
                qkv_unit(j, 0, 0)
            later_weights(0)
            y_back(0)
            for r in range(NT):
                sp.wait_ge(h_ready, 4 + r + 1)
                sp.dma_start(h_dram[r], h[:, r, :]).then_inc(h_saved, 16)
            router_weights(1)
            with sp.Fori(0, 5) as chunk:
                for j in range(3, 6):
                    qkv_unit(j, chunk, chunk)
                for j in range(6, 9):
                    qkv_unit(j, chunk, chunk + 1)
            for j in range(3, 6):
                qkv_unit(j, 5, 5)
            for j in range(4):
                dense(U_O + j, 0, w_o_v[:, 4 * (j % 2):4 * (j % 2) + 4, 512 * (j // 2):512 * (j // 2) + 512])
            sp.wait_ge(x_lo, 16)
            sp.dma_start(h[:, :, :], h_dram.rearrange("r p d -> p r d")).then_inc(h_back, 16)
            norm_gain(3)
            gate_up(1, 0, 0, 0)
            store_rows(12)
            norm_gain(4)
            later_weights(1)
            y_back(1)
            for r in range(NT):
                sp.wait_ge(hn_ready, 16 + r + 1)
                sp.dma_start(out_v[:, r, :], hn[r % 2][:, :]).then_inc(out_stored[r % 2], 16)
            for stored in out_stored:
                sp.wait_ge(stored, 32)

        @block.gpsimd
        def _(pool):
            steps = [0]

            def after(ins):
                steps[0] += 1
                ins.then_inc(pool_step, 1)
                pool.wait_ge(pool_step, steps[0])

            def rstd_tile(first, r):
                pool.wait_ge(ssq_ready, first + r + 1)
                after(pool.tensor_scalar(msq[:, r:r + 1], ssq[:, r:r + 1], 1.0 / D, EPS, ALU.mult, ALU.add))
                pool.tensor_tensor(rstd[:, r:r + 1], msq[:, r:r + 1], neghalf[:, :], ALU.pow).then_inc(rstd_ready, 1)

            def rstd_tiles(first):
                for r in range(NT):
                    rstd_tile(first, r)

            after(pool.memset(ident[:, :], 0.0))
            after(pool.affine_select(out=ident[:, :], in_=ident[:, :], compare_op=ALU.not_equal, fill=1.0, base=0,
                                     pattern=[[-1, P]], channel_multiplier=1))
            pool.memset(ones[:, :], 1.0)
            after(pool.memset(neghalf[:, :], -0.5))
            after(pool.affine_select(out=below[:, :], in_=ones[:, :], compare_op=ALU.is_gt, fill=0.0, base=0,
                                     pattern=[[1, P]], channel_multiplier=-1))
            inv = (np.float32(ROPE_THETA) ** (-np.arange(0, HD, 2, dtype=np.float32) / np.float32(HD))).astype(np.float32)
            for j in range(32):
                last = pool.memset(inv_f[:, j:j + 1], float(inv[j]))
            last.then_inc(consts_ready, 1)
            pool.memset(u_pad[:, :, :, 0:1], 0.0)
            for j in range(4):
                pool.memset(rank4[:, j:j + 1], float(4 - j))
            for e in range(NE):
                pool.memset(exp512[:, e:e + 1], float(S * e))
            pool.iota(iota_f[:, :], pattern=[[1, P]], base=0, channel_multiplier=0, allow_small_or_imprecise_dtypes=True)
            pool.iota(dest_id[:, :, :], pattern=[[S, 2], [P, NT]], base=-2 * S, channel_multiplier=1, allow_small_or_imprecise_dtypes=True)
            pool.iota(cand_c[:, :], pattern=[[0, 1]], base=0, channel_multiplier=1, allow_small_or_imprecise_dtypes=True)
            pool.iota(row_i[:, :], pattern=[[0, 1]], base=0, channel_multiplier=1)
            pool.iota(dil0[:, :, :], pattern=[[0, 32], [1, 4]], base=0, channel_multiplier=0,
                      allow_small_or_imprecise_dtypes=True).then_inc(consts_ready, 1)
            rstd_tiles(0)
            after(pool.memset(mask[:, :, :], 0.0))
            for r in range(NT):
                win = mask[:, r, 0:S].rearrange("p (q b) -> p q b", q=NT)
                after(pool.affine_select(out=win, in_=win, compare_op=ALU.is_ge, fill=NEG, base=r,
                                         pattern=[[-1, NT], [-4, P]], channel_multiplier=4))
                after(pool.affine_select(out=win, in_=win, compare_op=ALU.is_ge, fill=NEG, base=P - r,
                                         pattern=[[1, NT], [4, P]], channel_multiplier=-4))
                last = pool.affine_select(out=mask[:, r, S:S + P], in_=mask[:, r, S:S + P], compare_op=ALU.is_ge,
                                          fill=NEG, base=0, pattern=[[-1, P]], channel_multiplier=1)
            pool.wait_ge(rows_ready, 1)
            for r in range(NT):
                last = pool.affine_select(out=mask[:, r, S + P:KEYS], in_=dil[:, :, :].rearrange("p b q -> p (b q)"),
                                          compare_op=ALU.is_ge, fill=NEG, base=0, pattern=[[-1, P]],
                                          channel_multiplier=1)
            last.then_inc(consts_ready, 1)

            def moe_rows(l):
                s = M[l]
                pool.wait_ge(x_lo, (8, 20)[l])
                pool.memset(x_rows[:, :], 0.0).then_inc(s["cleared"], 1)
                pool.wait_ge(s["cleared"], 1)
                pool.wait_ge(routed, 2 * l + 2)
                for stored in hn_stored:
                    pool.wait_ge(stored, 32 * (l + 1))
                pool.indirect_dma_start(x_rows[:, :], None, hn_dram,
                                        bass.IndirectOffsetOnAxis(ap=tok_list[:, 0:1], axis=0),
                                        bounds_check=S - 1, oob_is_err=False
                                        ).then_inc(s["rows_in"], 16)
                n = later_items(pool) + 1

                def block_of(i):
                    return pool.value_load(items[0:1, bass.ds(i, 1)], min_val=0, max_val=CAND - 1)

                def gather(i):
                    pool.tensor_copy(tok_col[:, :], tok_list[:, bass.ds(block_of(i), 1)]).then_inc(s["col"], 1)
                    pool.wait_ge(s["col"], i)
                    pool.sem_inc(pool_passed, 1)
                    pool.indirect_dma_start(x_rows[:, :], None, hn_dram,
                                            bass.IndirectOffsetOnAxis(ap=tok_col[:, 0:1], axis=0),
                                            bounds_check=S - 1, oob_is_err=False
                                            ).then_inc(s["rows_in"], 16)

                def store(i):
                    pool.wait_ge(s["y"], i + 2)
                    pool.tensor_copy(dest_col[:, :], dest_list[:, bass.ds(block_of(i), 1)]).then_inc(s["dest"], 1)
                    pool.wait_ge(s["dest"], i + 1)
                    pool.sem_inc(pool_passed, 1)
                    pool.indirect_dma_start(y_dram, bass.IndirectOffsetOnAxis(ap=dest_col[:, 0:1], axis=0),
                                            y_rows[:, :], None, bounds_check=2 * S - 1, oob_is_err=False
                                            ).then_inc(s["ystored"], 16)

                pool.wait_ge(s["turned"], 1)
                gather(1)
                pool.wait_ge(s["turned"], 2)
                gather(2)
                with pool.Fori(2, n) as i:
                    pool.wait_ge(s["turned"], i + 1)
                    gather(i + 1)
                    store(i - 2)
                store(n - 2)
                store(n - 1)

            def rope_sum(g4):
                for r in range(NT):
                    pool.wait_ge(rope_in, g4 + r + 1)
                    pool.wait_ge(qk_turned, g4 + r + 1)
                    pool.tensor_tensor(qk_rot[:, r, :], rope_a[r % 2][:, :], rope_b[r % 2][:, :], ALU.add
                                       ).then_inc(rope_added, 1)

            rstd_tiles(4)
            moe_rows(0)
            rstd_tiles(8)
            with pool.Fori(0, 2) as s:
                with pool.Fori(0, NATT) as g:
                    for p in range(2):
                        rope_sum((s * 6 + g * 2 + p) * 4)
                pool.wait_ge(h_saved, 16 * NT)
                pool.wait_ge(rope_added, s * 24 + 24 + 2)
                pool.wait_ge(qkT_ready, s * 24 + 24 + 4)
                pool.sem_inc(pool_passed, 1)
                pool.memset(q_pad[0][HD:P, :, :], 0.0)
                pool.memset(q_pad[1][0:HD, :, :], 0.0).then_inc(pads_cleared, 1)
            rstd_tiles(12)
            moe_rows(1)
            rstd_tiles(16)

        @block.scalar
        def _(act):
            def hi(uc, rev=0):
                act.wait_ge(raw_in[uc % RAW], rev * 32 + (uc // RAW + 1) * 16)
                act.wait_ge(unit_done, rev * 6 + uc + 1)
                act.activation(W_hi[uc % SPLIT][:, :, :], raw[uc % RAW][:, :, :], ACT.Copy).then_inc(split_hi, 1)

            def square(r, first, ready, count):
                act.wait_ge(ready, count)
                if first + r:
                    act.wait_ge(ssq_ready, first + r)
                act.activation(square_out[:, :], h[:, r, :], ACT.Square,
                               accum_out=ssq[:, r:r + 1]).then_inc(ssq_ready, 1)

            def turn_hi(stage, r):
                act.wait_ge(x_turned, 4 * min(stage, 3) + r + 1)
                act.activation(xT_hi_all[:, :, r * P:(r + 1) * P],
                               ps[:, 2 * r:2 * r + 2, :].rearrange("p a (k n) -> p (a k) n", n=P), ACT.Copy
                               ).then_inc(x_hi, 1)

            def squares_and_turn(stage, first, ready):
                for r in range(NT):
                    if r == NT - 1:
                        turn_hi(stage, 0)
                    square(r, first, *ready(r))
                for r in range(1, NT):
                    if stage == 0 and r == 2:
                        hi(0)
                    turn_hi(stage, r)

            def m_hi(l, c, rev):
                s = M[l]
                act.wait_ge(s["raw_in"][c % MRAW], rev * 16 + (c // MRAW + 1) * 16)
                act.wait_ge(s["done"], rev * 6 + c + 1)
                act.activation(MW_hi[c % MSPLIT][:, :, :], m_raw[c % MRAW][:, :, :], ACT.Copy).then_inc(s["hi"], 1)

            def experts_begin(l):
                act.wait_ge(unit_done, SPLIT + (U_QKV if l == 0 else U_END))
                for c in range(MSPLIT):
                    m_hi(l, c, 0)
                act.wait_ge(ex_in, 2 * l + 1)
                act.activation(t4[:, :, :], t4[:, :, :], ACT.Exp).then_inc(ex_out, 1)
                act.wait_ge(ex_in, 2 * l + 2)
                act.activation(ex[:, :], ex[:, :], ACT.Exp).then_inc(ex_out, 1)

            def experts(l):
                s = M[l]

                def rows_hi(i):
                    act.wait_ge(s["turned"], i + 1)
                    act.activation(xT_hi_all[:, 0:2, :].rearrange("p a n -> p (a n)"),
                                   ps[:, 2:4, :].rearrange("p a n -> p (a n)"), ACT.Copy).then_inc(s["xhi"], 1)

                def silu(i, unit):
                    act.wait_ge(s["done"], unit + MSPLIT + 1)
                    act.activation(silu_g[:, :], ps[:, 0, :], ACT.Silu).then_inc(s["silu"], 1)

                def act_hi(i):
                    act.wait_ge(s["aturned"], i + 1)
                    act.activation(xT_hi_all[:, 2, :], ps[:, 4, :], ACT.Copy).then_inc(s["ahi"], 1)

                def y_out(unit, stored):
                    act.wait_ge(s["done"], unit + MSPLIT + 1)
                    if stored is not None:
                        act.wait_ge(s["ystored"], stored)
                    act.activation(y_rows[:, :], ps[:, 5:7, :].rearrange("p a n -> p (a n)"), ACT.Copy
                                   ).then_inc(s["y"], 1)

                rows_hi(0)
                m_hi(l, 3, 0)
                silu(0, 1)
                m_hi(l, 4, 0)
                m_hi(l, 5, 0)
                act.wait_ge(s["done"], MSPLIT + 4)
                rows_hi(1)
                act.wait_ge(routed, 2 * l + 2)
                later = later_items(act)
                before_last = act.value_load(items[0:1, ITEM_COLS + 1:ITEM_COLS + 2], min_val=MIN_ITEMS - 2,
                                             max_val=MAX_ITEMS - 2)

                def step(i, y_before=True, stored=None):
                    m_hi(l, 6, i)
                    if y_before:
                        y_out(i * 6 + 3, stored)
                    act_hi(i)
                    m_hi(l, 7, i)
                    silu(i + 1, i * 6 + 5)
                    m_hi(l, 8, i)
                    m_hi(l, 9, i)
                    rows_hi(i + 2)
                    m_hi(l, 10, i)
                    m_hi(l, 11, i)

                step(0, y_before=False)
                step(1)
                with act.Fori(1, before_last) as before:
                    step(before + 1, stored=before * 16)
                y_out(later * 6 + 3, before_last * 16)
                act_hi(later)
                y_out(later * 6 + 5, later * 16)

            squares_and_turn(0, 0, lambda r: (x_in[r], 16))
            hi(1)
            act.wait_ge(trig_ready, 1)
            act.activation(trig[:, :, :, :], red[:, :, :, :], ACT.Sin).then_inc(trig_done, 1)
            with act.Fori(0, 2) as c:
                for q in range(3):
                    hi(2 * q + 2, c)
                    for b in range(4):
                        if q == 0:
                            wait_in_block(act, c, 0, b)
                            act.activation(c_gate[:, b, :], ps[:, b, :], ACT.Copy).then_inc(c_ready, 1)
                        if q == 2:
                            act.wait_ge(gated, c * 4 + b + 1 + 4)
                            act.activation(mixT_hi[:, bass.ds(c * 4 + b, 1), :].rearrange("p a n -> p (a n)"),
                                           conv_o[:, b, :], ACT.Copy).then_inc(mix_hi, 1)
                    hi(2 * q + 3, c)
            hi(14)
            hi(15)
            squares_and_turn(1, 4, lambda r: (h_ready, r + 1))
            experts_begin(0)
            experts(0)
            hi(U_QKV)
            hi(U_QKV + 1)
            squares_and_turn(2, 8, lambda r: (h_ready, 4 + r + 1))

            def softmax_exp(w, s32):
                act.wait_ge(masked, s32 + w + 1 + 2)
                act.activation(prob[w % 2][:, :], prob[w % 2][:, :], ACT.Exp, bias=neg_max[:, w:w + 1],
                               scale=-1.0, accum_out=denom[:, w:w + 1]).then_inc(expd, 1)

            def pad_q(n, s):
                rows = slice(HD * (n % 2), HD * (n % 2) + HD)
                if n >= 2:
                    act.wait_ge(scored, s * 32 + 4 * (n - 1))
                act.activation(q_pad[n % 2][rows, :, :], qkT[rows, :, 0, n // 2, :], ACT.Copy).then_inc(q_padded, 1)

            def store_heads(hb, s):
                act.wait_ge(pv_done, s * 32 + 8 * hb + 8)
                act.activation(oT[:, bass.ds(s * O_HALF + hb * S, S)], ps[:, 6, :], ACT.Copy).then_inc(o_stored, 1)

            with act.Fori(0, 2) as s:
                with act.Fori(0, NATT) as g:
                    for p in range(3):
                        rev = s * 3 + g
                        hi(U_QKV + 2 * p + 2, rev)
                        if p > 0:
                            g4 = (s * 6 + g * 2 + p - 1) * 4
                            for r in range(NT):
                                act.wait_ge(qk_turned, g4 + r + 1 + 4)
                                act.activation(
                                    qkT[:, bass.ds(g, 1), p - 1, :, r * P:(r + 1) * P].rearrange("p a b n -> p (a b) n"),
                                    ps[:, 4 + r, :].rearrange("p (b n) -> p b n", b=4), ACT.Copy
                                ).then_inc(qkT_ready, 1)
                        if p == 2:
                            for r in range(NT):
                                wait_qkv(act, rev, 2, r)
                                act.activation(v_all[:, bass.ds(g, 1), r, :].rearrange("p a n -> p (a n)"),
                                               ps[:, r, :], ACT.Copy).then_inc(v_ready, 1)
                        hi(U_QKV + 2 * p + 3, rev)
                s32 = s * 32
                act.wait_ge(qkT_ready, s * 24 + 24 + 4)
                act.wait_ge(pads_cleared, s + 1)
                pad_q(0, s)
                softmax_exp(0, s32)
                for w in range(32):
                    if w + 1 < 32:
                        softmax_exp(w + 1, s32)
                    if w % 8 == 0 and w:
                        store_heads(w // 8 - 1, s)
                    act.wait_ge(p_turned, s32 + w + 1 + 2)
                    act.activation(probT[:, 0:512], ps[:, 4, :], ACT.Copy).then_inc(pt_a, 1)
                    if w % NT == 1 and w // NT < 7:
                        pad_q(w // NT + 1, s)
                store_heads(3, s)
            act.wait_ge(o_stored, 9)
            for j in range(4):
                act.activation(xT_hi_all[:, 2 * j:2 * j + 2, :].rearrange("p a n -> p (a n)"), out_blocks(j), ACT.Copy
                               ).then_inc(x_hi, 1)
            hi(54)
            hi(55)
            squares_and_turn(4, 12, lambda r: (h_ready, 8 + r + 1))
            experts_begin(1)
            experts(1)
            for r in range(NT):
                square(r, 16, h_ready, 12 + r + 1)

        @block.vector
        def _(dve):
            steps = [0]

            def after(ins):
                steps[0] += 1
                ins.then_inc(dve_step, 1)
                dve.wait_ge(dve_step, steps[0])

            def lo(uc, rev=0):
                dve.wait_ge(split_hi, rev * 6 + uc + 1)
                dve.tensor_tensor(W_lo[uc % SPLIT][:, :, :], raw[uc % RAW][:, :, :],
                                  W_hi[uc % SPLIT][:, :, :].bitcast(F), ALU.subtract).then_inc(split_lo, 1)

            def residual_add(which, u0):
                for c in range(2):
                    for r in range(NT):
                        if r < 3:
                            dve.wait_ge(proj_done, 6 * which + 3 * c + r + 1)
                        else:
                            dve.wait_ge(unit_done, SPLIT + u0 + 2 * c + 2)
                        cols = slice(512 * c, 512 * c + 512)
                        ins = dve.tensor_tensor(h[:, r, cols], ps[:, 4 * c + r, :], h[:, r, cols], ALU.add)
                        if c == 1:
                            ins.then_inc(h_ready, 1)

            def norm_row(k, first, r):
                dve.wait_ge(gain_in, 16 * (k + 1))
                dve.wait_ge(rstd_ready, first + r + 1)
                if r >= 2:
                    if first < 16:
                        dve.wait_ge(x_turned, first + r - 1)
                    if first in (4, 12):
                        dve.wait_ge(hn_stored[r % 2], (32 if first == 12 else 0) + 16)
                    if first == 16:
                        dve.wait_ge(out_stored[r % 2], 16)
                if first < 16:
                    o = hn[r % 2][:, :].rearrange("p (k q) -> p k q", k=KD)
                    i0 = h[:, r, :].rearrange("p (q k) -> p k q", k=KD)
                    i1 = gain[:, :].rearrange("p (q k) -> p k q", k=KD)
                else:
                    o, i0, i1 = hn[r % 2][:, :], h[:, r, :], gain[:, :]
                dve.scalar_tensor_tensor(out=o, in0=i0, scalar=rstd[:, r:r + 1], in1=i1, op0=ALU.mult,
                                         op1=ALU.mult).then_inc(hn_ready, 1)

            def turn_lo(stage, r):
                dve.wait_ge(x_hi, 4 * stage + r + 1)
                sl = slice(r * P, (r + 1) * P)
                dve.tensor_tensor(xT_lo_all[:, :, sl],
                                  ps[:, 2 * r:2 * r + 2, :].rearrange("p a (k n) -> p (a k) n", n=P),
                                  xT_hi_all[:, :, sl].bitcast(F), ALU.subtract).then_inc(x_lo, 1)

            def norm_and_turn(k, first, stage, made):
                for r in range(made, NT):
                    norm_row(k, first, r)
                    if r == NT - 1 and stage == 0:
                        lo(0)
                    if r >= 1:
                        turn_lo(stage, r - 1)
                turn_lo(stage, NT - 1)

            def router_split(l):
                dve.wait_ge(router_in, 16 * 7 * (l + 1))
                dve.tensor_copy(wr[:, :, 0:NG], wc_raw[:, :, :])
                after(dve.tensor_copy(wr[:, :, NG:20].rearrange("p k (g e) -> p k g e", g=NG),
                                      wf_raw[:, :, :, :].rearrange("p g k e -> p k g e")))
                after(dve.tensor_copy(wr2[:, :, 0:20], wr[:, :, :]))
                dve.tensor_tensor(wr2[:, :, 20:40], wr[:, :, :], wr2[:, :, 0:20].bitcast(F), ALU.subtract
                                  ).then_inc(wr_ready, 1)

            def bc(ap, n):
                return ap.unsqueeze(len(ap.shape)).to_broadcast(list(ap.shape) + [n])

            def first_max(o, vals, mx):
                after(dve.tensor_reduce(mx[:, :], vals, AX.X, ALU.max))
                after(dve.tensor_tensor(o, vals, bc(mx[:, :], 4), ALU.is_equal))
                after(dve.tensor_tensor(o, o, rank4[:, :].unsqueeze(1).to_broadcast([P, NT, 4]), ALU.mult))
                after(dve.tensor_reduce(rs[:, :], o, AX.X, ALU.max))
                after(dve.tensor_tensor(o, o, bc(rs[:, :], 4), ALU.is_equal))

            def route(l):
                dve.wait_ge(logits_done, l + 1)
                dve.tensor_copy(lgT[:, :], ps[0:40, 6, :]).then_inc(logits_copied, 1)
                dve.wait_ge(logits_turned, l + 1)
                parts = ps[:, 4, 0:40 * NT].rearrange("p (r n) -> p r n", r=NT)
                after(dve.tensor_tensor(lg[:, :, :], parts[:, :, 20:40],
                                        bias_r[:, :].unsqueeze(1).to_broadcast([P, NT, 20]), ALU.add))
                after(dve.tensor_tensor(lg[:, :, :], parts[:, :, 0:20], lg[:, :, :], ALU.add))
                coarse = lg[:, :, 0:NG]
                first_max(oh_g[:, :, :], coarse, m1)
                dve.tensor_tensor(t4[:, :, :], coarse, bc(m1[:, :], 4), ALU.subtract).then_inc(ex_in, 1)
                after(dve.tensor_tensor(t16[:, :, :, :], lg[:, :, NG:20].rearrange("p r (g e) -> p r g e", g=NG),
                                        bc(oh_g[:, :, :], NPG), ALU.mult))
                after(dve.tensor_reduce(fsel[:, :, :], t16[:, :, :, :].rearrange("p r g e -> p r e g"), AX.X, ALU.add))
                first_max(o1[:, :, :], fsel[:, :, :], m1)
                after(dve.scalar_tensor_tensor(out=fsel[:, :, :], in0=o1[:, :, :], scalar=NEG, in1=fsel[:, :, :],
                                               op0=ALU.mult, op1=ALU.add))
                first_max(o2[:, :, :], fsel[:, :, :], m2)
                dve.wait_ge(ex_out, 2 * l + 1)
                dve.tensor_tensor(ex[:, :], m2[:, :], m1[:, :], ALU.subtract).then_inc(ex_in, 1)
                after(dve.tensor_reduce(rs[:, :], t4[:, :, :], AX.X, ALU.add))
                after(dve.reciprocal(ptop[:, :], rs[:, :]))
                for o, ee in ((o1, e1), (o2, e2)):
                    last = dve.tensor_tensor(ee[:, :, :, :], bc(oh_g[:, :, :], NPG),
                                             o[:, :, :].unsqueeze(2).to_broadcast([P, NT, NG, NPG]), ALU.mult)
                after(last)
                dve.tensor_tensor(used[:, :, :], e1[:, :, :, :].rearrange("p r g e -> p r (g e)"),
                                  e2[:, :, :, :].rearrange("p r g e -> p r (g e)"), ALU.add).then_inc(used_ready, 1)
                dve.wait_ge(used_ready, 2 * l + 1)
                after(dve.tensor_reduce(row_count[:, :], used[:, :, :].rearrange("p r e -> p e r"), AX.X, ALU.add))
                dve.tensor_copy(row_counts[:, :, :], row_count[:, :].unsqueeze(1).to_broadcast([P, NT, NE])
                                ).then_inc(used_ready, 1)
                dve.wait_ge(ex_out, 2 * l + 2)
                after(dve.tensor_scalar(rs[:, :], ex[:, :], 1.0, None, ALU.add))
                after(dve.reciprocal(rs[:, :], rs[:, :]))
                after(dve.tensor_tensor(gates[:, 0, :], ptop[:, :], rs[:, :], ALU.mult))
                after(dve.tensor_tensor(gates[:, 1, :], gates[:, 0, :], ex[:, :], ALU.mult))
                dve.wait_ge(pos_done, l + 1)
                after(dve.tensor_tensor(used[:, :, :], ps[:, 5, 0:64].rearrange("p (r e) -> p r e", r=NT),
                                        exp512[:, :].unsqueeze(1).to_broadcast([P, NT, NE]), ALU.add))
                for c, ee in enumerate((e1, e2)):
                    ev = ee[:, :, :, :].rearrange("p r g e -> p r (g e)")
                    after(dve.tensor_tensor(ev, ev, used[:, :, :], ALU.mult))
                    last = dve.tensor_reduce(slot_f[:, c, :], ev, AX.X, ALU.add)
                after(last)
                after(dve.tensor_copy(slot_i[:, :, :], slot_f[:, :, :]))
                dve.tensor_scalar(lane_i[:, :, :], slot_i[:, :, :], P - 1, None, ALU.bitwise_and)
                dve.tensor_scalar(exp_i[:, :, :], slot_i[:, :, :], 9, None, ALU.arith_shift_right)
                after(dve.tensor_scalar(blk_i[:, :, :], slot_i[:, :, :], 7, NT - 1, ALU.arith_shift_right,
                                        ALU.bitwise_and))
                dve.tensor_copy(lane_f[:, :, :], lane_i[:, :, :])
                dve.tensor_copy(slot_f[:, :, :], exp_i[:, :, :])
                after(dve.tensor_copy(cand_f[:, :, :], blk_i[:, :, :]))
                after(dve.scalar_tensor_tensor(out=cand_f[:, :, :], in0=cand_f[:, :, :], scalar=float(NE),
                                               in1=slot_f[:, :, :], op0=ALU.mult, op1=ALU.add))
                dve.tensor_scalar(valid[0:CAND, :], ps[0:CAND, 6, 0:1], cand_j[0:CAND, :], None, ALU.is_gt
                                  ).then_inc(valid_ready, 1)
                for n in range(8):
                    r, c = n // 2, n % 2
                    if n == 4:
                        dve.wait_ge(rank_done, l + 1)
                        dve.wait_ge(valid_ready, l + 1)
                        after(dve.tensor_copy(item_v[:, :], ps[0:CAND, 7, 0:1]))
                        dve.tensor_scalar(item_oh[:, 0:ITEM_COLS], iota_f[0:CAND, 0:ITEM_COLS], item_v[:, :],
                                          valid[0:CAND, :], ALU.is_equal, ALU.mult).then_inc(item_oh_ready, 1)
                    if n >= 2:
                        dve.wait_ge(list_step, 8 * l + n - 1)
                    dve.tensor_scalar(lane_oh[n % 2][:, :], iota_f[:, :], lane_f[:, c, r:r + 1], None, ALU.is_equal)
                    dve.tensor_scalar(blk_oh[n % 2][:, :], iota_f[:, 0:CAND], cand_f[:, c, r:r + 1],
                                      dest_id[:, c, r:r + 1], ALU.is_equal, ALU.mult).then_inc(onehots, 1)
                dve.wait_ge(items_done, l + 1)
                dve.tensor_scalar(items[:, ITEM_COLS:ITEM_COLS + 1], ps[0:1, 6, 64 + ITEM_COLS:65 + ITEM_COLS],
                                  -1.0, None, ALU.add)
                dve.tensor_scalar(items[:, ITEM_COLS + 1:], ps[0:1, 6, 64 + ITEM_COLS:65 + ITEM_COLS],
                                  -2.0, None, ALU.add)
                dve.tensor_copy(items[:, 0:ITEM_COLS], ps[0:1, 6, 64:64 + ITEM_COLS]).then_inc(routed, 1)
                dve.wait_ge(list_step, 8 * l + 8)
                after(dve.tensor_scalar(dest_list[:, :], ps[:, 5, 128:128 + CAND], float(2 * S), None, ALU.add))
                dve.tensor_scalar(tok_list[:, :], dest_list[:, :], 2 * S + S - 1, None, ALU.bitwise_and
                                  ).then_inc(routed, 1)

            def m_lo(l, c, rev):
                s = M[l]
                dve.wait_ge(s["hi"], rev * 6 + c + 1)
                dve.tensor_tensor(MW_lo[c % MSPLIT][:, :, :], m_raw[c % MRAW][:, :, :],
                                  MW_hi[c % MSPLIT][:, :, :].bitcast(F), ALU.subtract).then_inc(s["lo"], 1)

            def experts(l):
                s = M[l]

                def rows_lo(i):
                    dve.wait_ge(s["xhi"], i + 1)
                    dve.tensor_tensor(xT_lo_all[:, 0:2, :].rearrange("p a n -> p (a n)"),
                                      ps[:, 2:4, :].rearrange("p a n -> p (a n)"),
                                      xT_hi_all[:, 0:2, :].rearrange("p a n -> p (a n)").bitcast(F),
                                      ALU.subtract).then_inc(s["xlo"], 1)

                def act_mul(i, unit):
                    dve.wait_ge(s["silu"], i + 1)
                    dve.wait_ge(s["done"], unit + MSPLIT + 1)
                    dve.tensor_tensor(act_row[:, :], ps[:, 1, :], silu_g[:, :], ALU.mult).then_inc(s["act"], 1)

                def act_lo(i):
                    dve.wait_ge(s["ahi"], i + 1)
                    dve.tensor_tensor(xT_lo_all[:, 2, :], ps[:, 4, :], xT_hi_all[:, 2, :].bitcast(F), ALU.subtract
                                      ).then_inc(s["alo"], 1)

                rows_lo(0)
                m_lo(l, 3, 0)
                m_lo(l, 4, 0)
                act_mul(0, 3)
                rows_lo(1)
                m_lo(l, 5, 0)
                dve.wait_ge(routed, 2 * l + 2)
                n = later_items(dve) + 1
                with dve.Fori(1, n) as i:
                    rev = i - 1
                    m_lo(l, 6, rev)
                    act_lo(i - 1)
                    for c in range(7, 10):
                        m_lo(l, c, rev)
                    act_mul(i, i * 6 + 1)
                    rows_lo(i + 1)
                    m_lo(l, 10, rev)
                    m_lo(l, 11, rev)
                act_lo(n - 1)

            def combine(l, k, first):
                for r in range(NT):
                    dve.wait_ge(M[l]["pick_in"][r], 32)
                    after(dve.scalar_tensor_tensor(out=h[:, r, :], in0=y_pick[2 * r][:, :], scalar=gates[:, 0, r:r + 1],
                                                   in1=h[:, r, :], op0=ALU.mult, op1=ALU.add))
                    dve.scalar_tensor_tensor(out=h[:, r, :], in0=y_pick[2 * r + 1][:, :],
                                             scalar=gates[:, 1, r:r + 1], in1=h[:, r, :], op0=ALU.mult,
                                             op1=ALU.add).then_inc(h_ready, 1)
                    if r >= 1:
                        norm_row(k, first, r - 1)
                    if r >= 2 and l == 0:
                        turn_lo(2, r - 2)
                norm_row(k, first, NT - 1)
                if l == 0:
                    turn_lo(2, NT - 2)
                    turn_lo(2, NT - 1)

            dve.sem_inc(split_lo, RAW)
            for l in range(2):
                dve.sem_inc(M[l]["lo"], MRAW)
            norm_and_turn(0, 0, 0, 0)
            dve.wait_ge(conv_t, 1)
            after(dve.tensor_copy(conv_c[:, :], ps[:, 7, 0:24]))
            lo(1)
            dve.wait_ge(pos_in, 16)
            dve.wait_ge(consts_ready, 1)
            after(dve.tensor_copy(pos_f[:, :], pos_i[:, :]))
            for r in range(NT):
                last = dve.tensor_scalar(ang[:, r, :], inv_f[:, :], pos_f[:, r:r + 1], None, ALU.mult)
            after(last)
            two_pi = 2 * np.pi
            p1 = 6.28125
            p2 = float(np.float32(np.floor((two_pi - p1) * 2 ** 18) / 2 ** 18))
            p3 = float(np.float32(two_pi - p1 - p2))
            for j, quarter in enumerate((0.0, 0.25)):
                after(dve.tensor_scalar(turns[:, j], ang[:, :, :], 1 / two_pi, quarter, ALU.mult, ALU.add))
                after(dve.tensor_copy(turns_i[:, j], turns[:, j]))
                after(dve.tensor_copy(turns[:, j], turns_i[:, j]))
                after(dve.scalar_tensor_tensor(out=red[:, j], in0=turns[:, j], scalar=-p1, in1=ang[:, :, :],
                                               op0=ALU.mult, op1=ALU.add))
                after(dve.scalar_tensor_tensor(out=red[:, j], in0=turns[:, j], scalar=-p2, in1=red[:, j],
                                               op0=ALU.mult, op1=ALU.add))
                after(dve.scalar_tensor_tensor(out=red[:, j], in0=turns[:, j], scalar=-p3, in1=red[:, j],
                                               op0=ALU.mult, op1=ALU.add))
                if j:
                    after(dve.tensor_scalar(red[:, j], red[:, j], float(np.pi / 2), None, ALU.add))
                ins = dve.tensor_scalar(red[:, j], red[:, j], 3.1415925, -3.1415925, ALU.min, ALU.max)
            ins.then_inc(trig_ready, 1)
            dve.wait_ge(trig_ready, 1)
            dve.wait_ge(consts_ready, 2)
            after(dve.tensor_scalar(row_m[:, :], row_i[:, :], 3, None, ALU.bitwise_and))
            after(dve.tensor_copy(row_mf[:, :], row_m[:, :]))
            after(dve.tensor_scalar(dil0[:, :, :], dil0[:, :, :], row_mf[:, :], None, ALU.is_equal))
            dve.tensor_scalar(dil[:, :, :], dil0[:, :, :], -NEG, NEG, ALU.mult, ALU.add).then_inc(rows_ready, 1)
            after(dve.tensor_scalar(row_m[:, :], row_i[:, :], 4, None, ALU.arith_shift_right))
            after(dve.tensor_copy(row_mf[:, :], row_m[:, :]))
            dve.tensor_scalar(cand_j[:, :], row_mf[:, :], float(P), -0.5, ALU.mult, ALU.add)
            dve.wait_ge(trig_done, 1)
            for half, sign in ((0, -1.0), (32, 1.0)):
                dve.tensor_copy(cos_t[:, :, half:half + 32], trig[:, 1])
                after(dve.tensor_scalar(sin_t[:, :, half:half + 32], trig[:, 0], sign, None, ALU.mult))
            router_split(0)
            base_step = steps[0]
            conv_chain = 5
            with dve.Fori(0, 2) as c:
                def link(ins, k):
                    ins.then_inc(dve_step, 1)
                    dve.wait_ge(dve_step, c * (4 * conv_chain) + (base_step + k + 1))
                for q in range(3):
                    lo(2 * q + 2, c)
                    for b in range(4):
                        if q == 1:
                            k = conv_chain * b
                            wait_in_block(dve, c, 1, b)
                            dve.wait_ge(c_ready, c * 4 + b + 1)
                            uv, cv = u_pad[:, b], conv_o[:, b, :].rearrange("p (r a) -> p r a", r=NT)
                            dve.tensor_tensor(uv[:, :, 1:1 + P], ps[:, b, :].rearrange("p (r a) -> p r a", r=NT),
                                              c_gate[:, b, :].rearrange("p (r a) -> p r a", r=NT), ALU.mult
                                              ).then_inc(u_ready, 1)
                            dve.wait_ge(u_ready, c * 4 + b + 1)

                            def tap(t):
                                return conv_c[:, bass.ds(c * 4 + (8 * t + b), 1)]

                            def add(o, i, t, k):
                                link(dve.scalar_tensor_tensor(out=o, in0=i, scalar=tap(t), in1=o, op0=ALU.mult,
                                                              op1=ALU.add), k)
                            link(dve.tensor_scalar(cv, uv[:, :, 1:1 + P], tap(2), None, ALU.mult), k)
                            add(cv[:, 1:4, :], uv[:, 0:3, 1:1 + P], 1, k + 1)
                            add(cv[:, 0, :], uv[:, 3, 0:P], 1, k + 2)
                            add(cv[:, 2:4, :], uv[:, 0:2, 1:1 + P], 0, k + 3)
                            add(cv[:, 0:2, :], uv[:, 2:4, 0:P], 0, k + 4)
                        if q == 2:
                            wait_in_block(dve, c, 2, b)
                            dve.tensor_tensor(conv_o[:, b, :], ps[:, b, :], conv_o[:, b, :], ALU.mult
                                              ).then_inc(gated, 1)
                    if q == 2:
                        for b in range(4):
                            dve.wait_ge(mix_hi, c * 4 + b + 1)
                            dst = mixT_lo[:, bass.ds(c * 4 + b, 1), :].rearrange("p a n -> p (a n)")
                            src = mixT_hi[:, bass.ds(c * 4 + b, 1), :].rearrange("p a n -> p (a n)").bitcast(F)
                            dve.tensor_tensor(dst, conv_o[:, b, :], src, ALU.subtract).then_inc(mix_lo, 1)
                    lo(2 * q + 3, c)
            steps[0] = base_step + 2 * 4 * conv_chain
            lo(14)
            lo(15)
            residual_add(0, U_OUT)
            norm_and_turn(1, 4, 1, 0)
            for c in range(2):
                m_lo(0, c, 0)
            route(0)
            m_lo(0, 2, 0)
            experts(0)
            lo(U_QKV)
            lo(U_QKV + 1)
            combine(0, 2, 8)
            router_split(1)
            dve.sem_inc(masked, 2)

            def mask_scores(w, s32):
                r = w % NT
                b = 2 * (w % 2)
                dve.wait_ge(scored, s32 + w + 1)
                dve.wait_ge(p_turned, s32 + w + 1)
                dve.sem_inc(dve_passed, 1)
                dve.tensor_tensor_reduce(out=prob[w % 2][:, :],
                                         in0=ps[:, b:b + 2, :].rearrange("p a n -> p (a n)")[:, 0:KEYS],
                                         in1=mask[:, r, :], scale=-SCALE, scalar=3e38, op0=ALU.add, op1=ALU.min,
                                         accum_out=neg_max[:, w:w + 1]).then_inc(masked, 1)

            def scale_probs(w, s32):
                dve.wait_ge(expd, s32 + w + 1)
                dve.reciprocal(inv_den[:, w:w + 1], denom[:, w:w + 1]).then_inc(inverted, 1)
                dve.wait_ge(inverted, s32 + w + 1)
                dve.tensor_scalar(prob[w % 2][:, :], prob[w % 2][:, :], inv_den[:, w:w + 1], None, ALU.mult
                                  ).then_inc(scaled, 1)

            with dve.Fori(0, 2) as s:
                with dve.Fori(0, NATT) as g:
                    for p in range(3):
                        rev = s * 3 + g
                        lo(U_QKV + 2 * p + 2, rev)
                        if p < 2:
                            g4 = (s * 6 + g * 2 + p) * 4
                            for r in range(NT):
                                wait_qkv(dve, rev, p, r)
                                dve.wait_ge(rope_added, g4 + r + 1)
                                t = ps[:, r, :].rearrange("p (h d) -> p h d", d=HD)
                                av = rope_a[r % 2][:, :].rearrange("p (h d) -> p h d", d=HD)
                                bv = rope_b[r % 2][:, :].rearrange("p (h d) -> p h d", d=HD)
                                cb = cos_t[:, r, :].unsqueeze(1).to_broadcast([P, 8, HD])
                                dve.tensor_tensor(av, t, cb, ALU.mult)
                                for x0, x1 in ((0, 32), (32, 0)):
                                    sb_ = sin_t[:, r, x0:x0 + 32].unsqueeze(1).to_broadcast([P, 8, 32])
                                    ins = dve.tensor_tensor(bv[:, :, x0:x0 + 32], t[:, :, x1:x1 + 32], sb_, ALU.mult)
                                ins.then_inc(rope_in, 1)
                        lo(U_QKV + 2 * p + 3, rev)
                s32 = s * 32
                mask_scores(0, s32)
                scale_probs(0, s32)
                for w in range(32):
                    if w + 1 < 32:
                        mask_scores(w + 1, s32)
                    dve.wait_ge(p_turned, s32 + w + 1 + 2)
                    dve.tensor_copy(probT[:, 512:KEYS], ps[:, 5, 0:256]).then_inc(pt_b, 1)
                    if w + 1 < 32:
                        scale_probs(w + 1, s32)
            for j in range(4):
                dve.wait_ge(x_hi, 12 + j + 1)
                dve.tensor_tensor(xT_lo_all[:, 2 * j:2 * j + 2, :].rearrange("p a n -> p (a n)"), out_blocks(j),
                                  xT_hi_all[:, 2 * j:2 * j + 2, :].rearrange("p a n -> p (a n)").bitcast(F),
                                  ALU.subtract).then_inc(x_lo, 1)
            lo(54)
            lo(55)
            dve.wait_ge(h_back, 16)
            residual_add(1, U_O)
            norm_and_turn(3, 12, 4, 0)
            for c in range(2):
                m_lo(1, c, 0)
            route(1)
            m_lo(1, 2, 0)
            experts(1)
            combine(1, 4, 16)

        @block.tensor
        def _(pe):
            def turn_rows(first):
                for r in range(NT):
                    pe.wait_ge(hn_ready, first + r + 1)
                    for k in range(KD):
                        rows = hn[r % 2][:, k * P:(k + 1) * P]
                        ins = pe.transpose(ps[:, 2 * r + k // 4, (k % 4) * P:(k % 4 + 1) * P], rows, ident[:, :])
                    ins.then_inc(x_turned, 1)

            def project(u0, xh, xl, split, halves):
                for c in range(2):
                    for kh in range(2):
                        u = u0 + 2 * c + kh
                        if c == 0:
                            pe.wait_ge(split, halves[kh])
                        pe.wait_ge(split_lo, RAW + u + 1)
                        for r in range(NT):
                            for k in range(4):
                                ins = product(pe, ps[:, 4 * c + r, :], xh[:, 4 * kh + k, r * P:(r + 1) * P],
                                              xl[:, 4 * kh + k, r * P:(r + 1) * P], W_hi[u % 2][:, k, :],
                                              W_lo[u % 2][:, k, :], kh == 0 and k == 0, kh == 1 and k == 3)
                            if kh == 1 and r < NT - 1:
                                ins.then_inc(proj_done, 1)
                        ins.then_inc(unit_done, 1)

            def router(l):
                pe.wait_ge(wr_ready, l + 1)
                pe.wait_ge(x_lo, (4 if l == 0 else 16) + 4)
                for k in range(KD):
                    for n, xt in enumerate((xT_hi_all, xT_lo_all)):
                        ins = pe.matmul(ps[0:40, 6, :], wr2[:, k, :], xt[:, k, :], start=(k == 0 and n == 0),
                                        stop=(k == KD - 1 and n == 1))
                ins.then_inc(logits_done, 1)
                pe.wait_ge(logits_copied, l + 1)
                for r in range(NT):
                    ins = pe.transpose(ps[:, 4, 40 * r:40 * r + 40], lgT[:, r * P:(r + 1) * P], ident[0:40, 0:40])
                ins.then_inc(logits_turned, 1)
                pe.wait_ge(used_ready, 2 * l + 1)
                pe.matmul(ps[:, 5, 0:NT * NE], below[:, :], used[:, :, :].rearrange("p r e -> p (r e)"), start=True,
                          stop=False)
                for q in range(NT - 1):
                    pe.matmul(ps[:, 5, NE * (q + 1):NT * NE], ones[:, :],
                              used[:, q, :].unsqueeze(1).to_broadcast([P, NT - 1 - q, NE]), start=False,
                              stop=(q == NT - 2))
                pe.wait_ge(used_ready, 2 * l + 2)
                pe.matmul(ps[0:CAND, 6, 0:1], row_counts[:, :, :].rearrange("p j e -> p (j e)"), ones[:, 0:1],
                          start=True, stop=True).then_inc(pos_done, 1)
                pe.wait_ge(valid_ready, l + 1)
                pe.matmul(ps[0:CAND, 7, 0:1], below[0:CAND, 0:CAND], valid[0:CAND, :], start=True, stop=True
                          ).then_inc(rank_done, 1)
                for n in range(8):
                    if n == 4:
                        pe.wait_ge(item_oh_ready, l + 1)
                        pe.matmul(ps[0:1, 6, 64:64 + ITEM_COLS], cand_c[0:CAND, :], item_oh[:, 0:ITEM_COLS],
                                  start=True, stop=True)
                        pe.matmul(ps[0:1, 6, 64 + ITEM_COLS:65 + ITEM_COLS], valid[0:CAND, :], ones[0:CAND, 0:1],
                                  start=True, stop=True).then_inc(items_done, 1)
                    pe.wait_ge(onehots, 8 * l + n + 1)
                    ins = pe.matmul(ps[:, 5, 128:128 + CAND], lane_oh[n % 2][:, :], blk_oh[n % 2][:, :],
                                    start=(n == 0), stop=(n == 7))
                    ins.then_inc(list_step, 1)

            def experts(l):
                s = M[l]
                xh = xT_hi_all[:, 0:2, :].rearrange("p a (k n) -> p (a k) n", n=P)
                xl = xT_lo_all[:, 0:2, :].rearrange("p a (k n) -> p (a k) n", n=P)
                ah, al = (t[:, 2, :].rearrange("p (k n) -> p k n", n=P) for t in (xT_hi_all, xT_lo_all))

                def turn_x(i):
                    pe.wait_ge(s["rows_in"], i * 16 + 16)
                    for k in range(KD):
                        ins = pe.transpose(ps[:, 2 + k // 4, (k % 4) * P:(k % 4 + 1) * P],
                                           x_rows[:, k * P:(k + 1) * P], ident[:, :])
                    ins.then_inc(s["turned"], 1)

                def turn_act(i):
                    pe.wait_ge(s["act"], i + 1)
                    for k in range(KF):
                        ins = pe.transpose(ps[:, 4, k * P:(k + 1) * P], act_row[:, k * P:(k + 1) * P], ident[:, :])
                    ins.then_inc(s["aturned"], 1)

                def up_unit(c, i6, j):
                    b = c % MSPLIT
                    pe.wait_ge(s["lo"], i6 + c + 1 + MRAW)
                    for k in range(4):
                        ins = product(pe, ps[:, j // 2, :], xh[:, 4 * (j % 2) + k, :], xl[:, 4 * (j % 2) + k, :],
                                      MW_hi[b][:, k, :], MW_lo[b][:, k, :], j % 2 == 0 and k == 0,
                                      j % 2 == 1 and k == 3)
                    ins.then_inc(s["done"], 1)

                def down_unit(c, i6, j):
                    b = c % MSPLIT
                    pe.wait_ge(s["lo"], i6 + c + 1 + MRAW)
                    for k in range(2):
                        for half in range(2):
                            ins = product(pe, ps[:, 5 + half, :], ah[:, 2 * j + k, :], al[:, 2 * j + k, :],
                                          MW_hi[b][:, 2 * k + half, :], MW_lo[b][:, 2 * k + half, :],
                                          j == 0 and k == 0, j == 1 and k == 1)
                    ins.then_inc(s["done"], 1)

                turn_x(0)
                pe.wait_ge(s["xlo"], 1)
                for j in range(3):
                    up_unit(j, 0, j)
                turn_x(1)
                up_unit(3, 0, 3)
                pe.wait_ge(routed, 2 * l + 2)
                n = later_items(pe) + 1
                with pe.Fori(1, n) as i:
                    i6 = i * 6 - 6
                    pe.wait_ge(s["xlo"], i + 1)
                    pe.wait_ge(s["act"], i)
                    up_unit(4, i6, 0)
                    turn_act(i - 1)
                    for j in range(1, 4):
                        up_unit(4 + j, i6, j)
                    turn_x(i + 1)
                    pe.wait_ge(s["alo"], i)
                    pe.wait_ge(s["y"], i)
                    down_unit(8, i6, 0)
                    down_unit(9, i6, 1)
                turn_act(n - 1)
                pe.wait_ge(s["alo"], n)
                pe.wait_ge(s["y"], n)
                down_unit(4, n * 6 - 6, 0)
                down_unit(5, n * 6 - 6, 1)

            pe.sem_inc(unit_done, SPLIT)
            pe.sem_inc(gated, 4)
            for l in range(2):
                pe.sem_inc(M[l]["done"], MSPLIT)
                pe.sem_inc(M[l]["y"], 1)
            pe.wait_ge(consts_ready, 1)
            turn_rows(0)
            pe.wait_ge(x_lo, 4)
            pe.wait_ge(conv_in, 16)
            pe.transpose(ps[:, 7, 0:24], conv_rows[:, :], ident[0:24, 0:24]).then_inc(conv_t, 1)
            with pe.Fori(0, 2) as c:
                for q in range(3):
                    for kh in range(2):
                        uc = 2 * q + kh
                        pe.wait_ge(split_lo, c * 6 + RAW + uc + 1)
                        for b in range(4):
                            if kh == 0:
                                pe.wait_ge((gated, c_ready, u_ready)[q], c * 4 + b + 1)
                            for k in range(4):
                                ws = slice(b * P, (b + 1) * P)
                                ins = product(pe, ps[:, b, :], W_hi[uc % 2][:, k, ws], W_lo[uc % 2][:, k, ws],
                                              xT_hi_all[:, 4 * kh + k, :], xT_lo_all[:, 4 * kh + k, :],
                                              kh == 0 and k == 0, kh == 1 and k == 3)
                            if kh == 1 and b < 3:
                                ins.then_inc(block_done, 1)
                        ins.then_inc(unit_done, 1)
            project(U_OUT, mixT_hi, mixT_lo, mix_lo, (5, 8))
            turn_rows(4)
            router(0)
            experts(0)
            turn_rows(8)
            pe.sem_inc(v_ready, 4)
            pe.sem_inc(rope_added, 2)
            pe.sem_inc(qk_turned, 4)
            pe.sem_inc(p_turned, 2)
            pe.sem_inc(pt_a, 1)
            pe.sem_inc(pt_b, 1)
            pe.sem_inc(o_stored, 1)
            pe.sem_inc(qkT_ready, 4)
            pe.wait_ge(consts_ready, 3)

            with pe.Fori(0, 2) as s:
                with pe.Fori(0, NATT) as g:
                    for p in range(3):
                        for kh in range(2):
                            uc, ui = U_QKV + 2 * p + kh, s * 18 + g * 6
                            pe.wait_ge(split_lo, ui + RAW + uc + 1)
                            for r in range(NT):
                                if kh == 0 and p == 0:
                                    pe.wait_ge(v_ready, (s * 3 + g) * 4 + r + 1)
                                    pe.wait_ge(x_lo, 8 + r + 1)
                                elif kh == 0:
                                    pe.wait_ge(rope_in, (s * 6 + g * 2 + p - 1) * 4 + r + 1)
                                for k in range(4):
                                    ins = product(pe, ps[:, r, :], xT_hi_all[:, 4 * kh + k, r * P:(r + 1) * P],
                                                  xT_lo_all[:, 4 * kh + k, r * P:(r + 1) * P],
                                                  W_hi[uc % 2][:, k, :], W_lo[uc % 2][:, k, :],
                                                  kh == 0 and k == 0, kh == 1 and k == 3)
                                if kh == 1 and r < NT - 1:
                                    ins.then_inc(qkv_done, 1)
                            ins.then_inc(unit_done, 1)
                            if kh == 0 and p > 0:
                                g4 = (s * 6 + g * 2 + p - 1) * 4
                                for r in range(NT):
                                    pe.wait_ge(rope_added, g4 + r + 1 + 2)
                                    pe.wait_ge(qkT_ready, g4 + r + 1)
                                    if r == 2:
                                        pe.wait_ge(o_stored, s * 4 + 1)
                                    for hb in range(4):
                                        tr = pe.transpose(ps[:, 4 + r, hb * P:(hb + 1) * P],
                                                          qk_rot[:, r, hb * P:(hb + 1) * P], ident[:, :])
                                    tr.then_inc(qk_turned, 1)
                s32 = s * 32
                pe.wait_ge(qkT_ready, s * 24 + 24 + 4)
                pe.wait_ge(v_ready, s * 12 + 12 + 4)

                def scores(w):
                    head, r = w // NT, w % NT
                    q, hb, b = q_pad[head % 2], head // 2, 2 * (w % 2)
                    if r == 0:
                        pe.wait_ge(q_padded, s * 8 + head + 1)
                    pe.wait_ge(masked, s32 + w + 1)
                    tile_r = slice(r * P, (r + 1) * P)
                    pe.matmul(ps[:, b, :], q[:, 0, tile_r], qkT[:, 0, 1, hb, :], start=True, stop=True)
                    pe.matmul(ps[:, b + 1, 0:P], q[:, 1, tile_r], qkT[:, 1, 1, hb, tile_r], start=True, stop=True)
                    pe.matmul(ps[:, b + 1, P:2 * P], q[:, 2, tile_r], qkT[:, 2, 1, hb, tile_r],
                              start=True, stop=True).then_inc(scored, 1)

                def weighted(w):
                    head, r = w // NT, w % NT
                    o = ps[HD * (head % 2):HD * (head % 2) + HD, 6, r * P:(r + 1) * P]
                    cols = slice(head * HD, head * HD + HD)
                    if w % 8 == 0:
                        pe.wait_ge(o_stored, s * 4 + w // 8 + 1)
                    pe.wait_ge(pt_a, s32 + w + 2)
                    pe.wait_ge(pt_b, s32 + w + 2)
                    keys = [(0, q) for q in range(NT)] + [(1, r), (2, r)]
                    for n, (g, q) in enumerate(keys):
                        ins = pe.matmul(o, v_all[:, g, q, cols], probT[:, n * P:(n + 1) * P], start=(n == 0),
                                        stop=(n == 5))
                    ins.then_inc(pv_done, 1)

                scores(0)
                for w in range(32):
                    if w + 1 < 32:
                        scores(w + 1)
                    if w:
                        weighted(w - 1)
                    pe.wait_ge(scaled, s32 + w + 1)
                    pe.wait_ge(pt_a, s32 + w + 1)
                    pe.wait_ge(pt_b, s32 + w + 1)
                    for n in range(6):
                        ins = pe.transpose(ps[:, 4 + n // 4, (n % 4) * P:(n % 4 + 1) * P],
                                           prob[w % 2][:, n * P:(n + 1) * P], ident[:, :])
                    ins.then_inc(p_turned, 1)
                weighted(31)
            project(U_O, xT_hi_all, xT_lo_all, x_lo, (14, 16))
            turn_rows(12)
            router(1)
            experts(1)


_INS = ["x", "positions", "norm_mix", "norm_ffn", "norm_final", "conv_w_in", "conv_w", "conv_w_out", "attn_w_qkv",
        "attn_w_o", "w_coarse", "b_coarse", "w_fine", "b_fine", "w_gate", "w_up", "w_down"]


def kernel(**inputs):
    import concourse.bacc as bacc
    from concourse.bass_utils import run_bass_kernel_spmd

    nc = bacc.Bacc("TRN2", target_bir_lowering=False, num_devices=1)
    arrays, args = {}, []
    for name in _INS:
        a = np.ascontiguousarray(inputs[name])
        arrays[f"in_{name}_dram"] = a
        args.append(nc.dram_tensor(f"in_{name}_dram", a.shape, mybir.dt.from_np(a.dtype), kind="ExternalInput").ap())
    out = nc.dram_tensor("out_0_dram", (1, S, D), F, kind="ExternalOutput").ap()
    build(nc, *args, out)
    r = run_bass_kernel_spmd(nc, [arrays], core_ids=[0])
    return r.results[0]["out_0_dram"]
```
